# Optimizing a Trainium2 kernel written in Bass

```python
import math
import jax, jax.numpy as jnp
from jax import lax
import numpy as np

D_MODEL = 1024
BATCH = 1
SEQ = 256
DEPTH = 1
DEC_BATCH = 1
DEC_SEQ = 512
PAST_LEN = 128

DIFF_HEADS = 4
DIFF_HEAD_DIM = 64
DIFF_WIDTH = DIFF_HEADS * 2 * DIFF_HEAD_DIM
NA_HEADS = 8
NA_HEAD_DIM = 64
NA_WIDTH = NA_HEADS * NA_HEAD_DIM
GRID_W = 64
NA_WIN_ROWS = 8
NA_WIN_COLS = 16
NA_QCB = NA_WIN_COLS
NA_KCB = 2 * NA_WIN_COLS
NA_NCB = GRID_W // NA_QCB
GATE_WIDTH = 2 * D_MODEL
IN_SPLITS = [DIFF_WIDTH, 2 * DIFF_WIDTH, 3 * DIFF_WIDTH, 3 * DIFF_WIDTH + NA_WIDTH, 3 * DIFF_WIDTH + 2 * NA_WIDTH, 3 * DIFF_WIDTH + 3 * NA_WIDTH]
IN_WIDTH = 3 * DIFF_WIDTH + 3 * NA_WIDTH + GATE_WIDTH
T5_BUCKETS = 32
T5_MAX_DIST = 128
Q_BLOCK = 128
N_EXPERTS = 16
EXPERT_FF = 2816
CAPACITY_FACTOR = 2
EPS = 1e-6

kernel_name = "hybrid_diffattn_natten_ec_encoder"

def rms_norm(x, g):
    x32 = x.astype(jnp.float32)
    y = x32 * lax.rsqrt(jnp.mean(x32 * x32, axis=-1, keepdims=True) + EPS)
    return (y * g.astype(jnp.float32)).astype(x.dtype)

def t5_bucket(rel):
    nb = T5_BUCKETS // 2
    max_exact = nb // 2
    side = jnp.where(rel > 0, nb, 0)
    n = jnp.abs(rel)
    nf = jnp.maximum(n, 1).astype(jnp.float32)
    large = max_exact + (jnp.log(nf / max_exact) / math.log(T5_MAX_DIST / max_exact) * (nb - max_exact)).astype(jnp.int32)
    large = jnp.minimum(large, nb - 1)
    return side + jnp.where(n < max_exact, n, large)

def diff_attention(q1, q2, k1, k2, v, lam, rel_bias):
    B, H, S, hd = q1.shape
    nb = S // Q_BLOCK
    kpos = jnp.arange(S, dtype=jnp.int32)
    table = rel_bias.astype(jnp.float32)

    def to_blocks(q):
        return jnp.moveaxis(q.reshape(B, H, nb, Q_BLOCK, hd), 2, 0)

    def block(args):
        qa, qb, i = args
        qpos = i * Q_BLOCK + jnp.arange(Q_BLOCK, dtype=jnp.int32)
        bias = jnp.transpose(table[t5_bucket(kpos[None, :] - qpos[:, None])], (2, 0, 1))
        p1 = jax.nn.softmax(jnp.einsum('bhqd,bhkd->bhqk', qa, k1).astype(jnp.float32) + bias, axis=-1)
        p2 = jax.nn.softmax(jnp.einsum('bhqd,bhkd->bhqk', qb, k2).astype(jnp.float32) + bias, axis=-1)
        a = (p1 - lam * p2).astype(v.dtype)
        return jnp.einsum('bhqk,bhke->bhqe', a, v)

    out = lax.map(block, (to_blocks(q1), to_blocks(q2), jnp.arange(nb, dtype=jnp.int32)))
    return jnp.moveaxis(out, 0, 2).reshape(B, H, S, v.shape[-1])

def na_column_structure():
    c = np.arange(GRID_W)
    col_start = np.clip(c - NA_WIN_COLS // 2, 0, GRID_W - NA_WIN_COLS).reshape(NA_NCB, NA_QCB)
    kblk_start = np.clip(np.arange(NA_NCB) * NA_QCB - NA_WIN_COLS // 2, 0, GRID_W - NA_KCB)
    kcol_idx = kblk_start[:, None] + np.arange(NA_KCB)[None, :]
    kc = kcol_idx[:, None, :]
    cs = col_start[:, :, None]
    col_valid = (kc >= cs) & (kc < cs + NA_WIN_COLS)
    dc = kc - c.reshape(NA_NCB, NA_QCB)[:, :, None]
    dc_idx = np.clip(dc + NA_WIN_COLS - 1, 0, 2 * NA_WIN_COLS - 2)
    return kcol_idx, col_valid, dc_idx

def neighborhood_attention(q, k, v, rpb):
    B, S, H, hd = q.shape
    rows = S // GRID_W
    wr = min(NA_WIN_ROWS, rows)
    kcol_idx, col_valid, dc_idx = na_column_structure()
    kg = k.reshape(B, rows, GRID_W, H, hd)
    vg = v.reshape(B, rows, GRID_W, H, hd)
    qg = jnp.moveaxis(q.reshape(B, rows, GRID_W, H, hd), 1, 0)
    table = rpb.astype(jnp.float32)
    mask = col_valid[:, :, None, :]

    def row_fn(args):
        q_row, r = args
        rs = jnp.clip(r - wr // 2, 0, rows - wr)
        k_blk = lax.dynamic_slice_in_dim(kg, rs, wr, axis=1)[:, :, kcol_idx]
        v_blk = lax.dynamic_slice_in_dim(vg, rs, wr, axis=1)[:, :, kcol_idx]
        qb = q_row.reshape(B, NA_NCB, NA_QCB, H, hd)
        logits = jnp.einsum('bjqhd,bwjkhd->bhjqwk', qb, k_blk).astype(jnp.float32)
        dr_idx = rs + jnp.arange(wr, dtype=jnp.int32) - r + (NA_WIN_ROWS - 1)
        bias = jnp.transpose(table[:, dr_idx][:, :, dc_idx], (0, 2, 3, 1, 4))
        logits = jnp.where(mask, logits + bias, -jnp.inf)
        p = jax.nn.softmax(logits, axis=(-2, -1)).astype(v.dtype)
        out = jnp.einsum('bhjqwk,bwjkhd->bjqhd', p, v_blk)
        return out.reshape(B, GRID_W, H, hd)

    out = lax.map(row_fn, (qg, jnp.arange(rows, dtype=jnp.int32)))
    return jnp.moveaxis(out, 0, 1).reshape(B, S, H, hd)

def token_mixer(x, lambda_init, norm_g, w_in, diff_qn, diff_kn, lq1, lk1, lq2, lk2, diff_subln, rel_bias,
                na_qn, na_kn, na_rpb, w_br_diff, w_br_na, w_out):
    B, S, _ = x.shape
    h = rms_norm(x, norm_g)
    proj = h @ w_in
    dq, dk, dv, nq, nk, nv, gates = jnp.split(proj, IN_SPLITS, axis=-1)
    dq = rms_norm(dq.reshape(B, S, DIFF_HEADS, 2, DIFF_HEAD_DIM), diff_qn) * (DIFF_HEAD_DIM ** -0.5)
    dk = rms_norm(dk.reshape(B, S, DIFF_HEADS, 2, DIFF_HEAD_DIM), diff_kn)
    q1 = jnp.transpose(dq[..., 0, :], (0, 2, 1, 3))
    q2 = jnp.transpose(dq[..., 1, :], (0, 2, 1, 3))
    k1 = jnp.transpose(dk[..., 0, :], (0, 2, 1, 3))
    k2 = jnp.transpose(dk[..., 1, :], (0, 2, 1, 3))
    dv = jnp.transpose(dv.reshape(B, S, DIFF_HEADS, 2 * DIFF_HEAD_DIM), (0, 2, 1, 3))
    f32 = jnp.float32
    lam = (jnp.exp(jnp.sum(lq1.astype(f32) * lk1.astype(f32))) - jnp.exp(jnp.sum(lq2.astype(f32) * lk2.astype(f32)))
           + lambda_init)
    o = diff_attention(q1, q2, k1, k2, dv, lam, rel_bias)
    o = rms_norm(o, diff_subln) * (1.0 - lambda_init)
    y_diff = jnp.transpose(o, (0, 2, 1, 3)).reshape(B, S, DIFF_WIDTH)
    nq = rms_norm(nq.reshape(B, S, NA_HEADS, NA_HEAD_DIM), na_qn) * (NA_HEAD_DIM ** -0.5)
    nk = rms_norm(nk.reshape(B, S, NA_HEADS, NA_HEAD_DIM), na_kn)
    nv = nv.reshape(B, S, NA_HEADS, NA_HEAD_DIM)
    y_na = neighborhood_attention(nq, nk, nv, na_rpb).reshape(B, S, NA_WIDTH)
    g_diff, g_na = jnp.split(jax.nn.sigmoid(gates), 2, axis=-1)
    merged = g_diff * (y_diff @ w_br_diff) + g_na * (y_na @ w_br_na)
    return x + merged @ w_out

def expert_choice_ffn(h, w_router, w_gate, w_up, w_down):
    B, S, D = h.shape
    n = B * S
    cap = CAPACITY_FACTOR * n // N_EXPERTS
    t = h.reshape(n, D)
    aff = jax.nn.softmax((t @ w_router).astype(jnp.float32), axis=-1)
    gate, idx = lax.top_k(aff.T, cap)

    def expert(args):
        wg, wu, wd, ix, g = args
        xe = t[ix]
        he = jax.nn.silu(xe @ wg) * (xe @ wu)
        return (he @ wd) * g[:, None].astype(he.dtype)

    ye = lax.map(expert, (w_gate, w_up, w_down, idx, gate))
    y = jnp.zeros((n, D), h.dtype).at[idx.reshape(-1)].add(ye.reshape(-1, D))
    return y.reshape(B, S, D)

def setup_inputs(seed: int = 0) -> dict:
    key = jax.random.key(seed)
    ks = jax.random.split(key, 24)
    f32 = jnp.float32

    def nrm(k, shape, scale):
        return scale * jax.random.normal(k, shape, f32)

    def gain(k, shape):
        return 1.0 + 0.02 * jax.random.normal(k, shape, f32)

    return {
        "x_prompt": nrm(ks[0], (BATCH, SEQ, D_MODEL), 1.0),
        "x_sample": nrm(ks[1], (DEC_BATCH, DEC_SEQ, D_MODEL), 1.0),
        "norm1_g": gain(ks[2], (DEPTH, D_MODEL)),
        "w_in": nrm(ks[3], (DEPTH, D_MODEL, IN_WIDTH), D_MODEL ** -0.5),
        "diff_q_norm": gain(ks[4], (DEPTH, DIFF_HEAD_DIM)),
        "diff_k_norm": gain(ks[5], (DEPTH, DIFF_HEAD_DIM)),
        "lambda_q1": nrm(ks[6], (DEPTH, DIFF_HEAD_DIM), 0.1),
        "lambda_k1": nrm(ks[7], (DEPTH, DIFF_HEAD_DIM), 0.1),
        "lambda_q2": nrm(ks[8], (DEPTH, DIFF_HEAD_DIM), 0.1),
        "lambda_k2": nrm(ks[9], (DEPTH, DIFF_HEAD_DIM), 0.1),
        "diff_subln_g": gain(ks[10], (DEPTH, 2 * DIFF_HEAD_DIM)),
        "rel_bias": nrm(ks[11], (T5_BUCKETS, DIFF_HEADS), 0.2),
        "na_q_norm": gain(ks[12], (DEPTH, NA_HEAD_DIM)),
        "na_k_norm": gain(ks[13], (DEPTH, NA_HEAD_DIM)),
        "na_rpb": nrm(ks[14], (DEPTH, NA_HEADS, 2 * NA_WIN_ROWS - 1, 2 * NA_WIN_COLS - 1), 0.2),
        "w_branch_diff": nrm(ks[15], (DEPTH, DIFF_WIDTH, D_MODEL), DIFF_WIDTH ** -0.5),
        "w_branch_na": nrm(ks[16], (DEPTH, NA_WIDTH, D_MODEL), NA_WIDTH ** -0.5),
        "w_out": nrm(ks[17], (DEPTH, D_MODEL, D_MODEL), D_MODEL ** -0.5),
        "norm2_g": gain(ks[18], (DEPTH, D_MODEL)),
        "w_router": nrm(ks[19], (DEPTH, D_MODEL, N_EXPERTS), D_MODEL ** -0.5),
        "w_expert_gate": nrm(ks[20], (DEPTH, N_EXPERTS, D_MODEL, EXPERT_FF), D_MODEL ** -0.5),
        "w_expert_up": nrm(ks[21], (DEPTH, N_EXPERTS, D_MODEL, EXPERT_FF), D_MODEL ** -0.5),
        "w_expert_down": nrm(ks[22], (DEPTH, N_EXPERTS, EXPERT_FF, D_MODEL), EXPERT_FF ** -0.5),
    }

def reference(x_prompt, x_sample, norm1_g, w_in, diff_q_norm, diff_k_norm, lambda_q1, lambda_k1, lambda_q2,
              lambda_k2, diff_subln_g, rel_bias, na_q_norm, na_k_norm, na_rpb, w_branch_diff, w_branch_na,
              w_out, norm2_g, w_router, w_expert_gate, w_expert_up, w_expert_down):
    def run(x):
        for l in range(DEPTH):
            lambda_init = 0.8 - 0.6 * math.exp(-0.3 * l)
            x = token_mixer(x, lambda_init, norm1_g[l], w_in[l], diff_q_norm[l], diff_k_norm[l],
                            lambda_q1[l], lambda_k1[l], lambda_q2[l], lambda_k2[l], diff_subln_g[l], rel_bias,
                            na_q_norm[l], na_k_norm[l], na_rpb[l], w_branch_diff[l], w_branch_na[l], w_out[l])
            x = x + expert_choice_ffn(rms_norm(x, norm2_g[l]), w_router[l], w_expert_gate[l],
                                      w_expert_up[l], w_expert_down[l])
        return x

    y_prompt = run(x_prompt)
    y_sample = run(x_sample)
    return (y_prompt, y_sample)


_drawn_inputs = setup_inputs


def setup_inputs(seed=0):
    import zlib

    import numpy as np

    out = dict(_drawn_inputs(seed))
    spreads = {}
    factors = {'norm1_g': 2.838,
     'diff_q_norm': 4.521,
     'diff_k_norm': 3.909,
     'lambda_q1': 3.732,
     'lambda_k2': 8.0,
     'diff_subln_g': 4.205,
     'na_q_norm': 8.0,
     'na_k_norm': 8.0,
     'na_rpb': 2.69,
     'norm2_g': 3.677}
    for name, (base, spread) in spreads.items():
        noise = np.random.default_rng([zlib.crc32(name.encode()), seed]).standard_normal(out[name].shape)
        drawn = base * np.exp(spread * noise) if base else spread * noise
        out[name] = __import__('jax').numpy.asarray(drawn.astype(out[name].dtype))
    for name, factor in factors.items():
        out[name] = (out[name] * factor).astype(out[name].dtype)
    return out
```

```python
import math
from contextlib import ExitStack

import concourse.bass as bass
from concourse import mybir

P = 128
D = 1024
SP_, SS = 256, 512
N = SP_ + SS
NT = N // P
KD = D // P
HW = 512
FF = 2816
E = 16
HF = FF // 2
FT = HF // P
CP, CS = 2 * SP_ // E, 2 * SS // E
CAP = CP + CS
EPS = 1e-6
LAM0 = 0.8 - 0.6 * math.exp(0.0)
BW = 896
NA_ROWS = 15
GROUPS = [(0, 2), (2, 4)]

F32 = mybir.dt.float32
I32 = mybir.dt.int32
ALU = mybir.AluOpType
ACT = mybir.ActivationFunctionType
AX = mybir.AxisListType

C_ID, C_MASK, C_TOK, C_SLOT, C_POW = 0, 128, 192, 198, 262
C_W = C_POW + 64


def encoder(nc, x_prompt, x_sample, norm1_g, w_in, diff_q_norm, diff_k_norm, lambda_q1, lambda_k1, lambda_q2,
            lambda_k2, diff_subln_g, rel_bias, na_q_norm, na_k_norm, na_rpb, w_branch_diff, w_branch_na, w_out,
            norm2_g, w_router, w_expert_gate, w_expert_up, w_expert_down, consts, t5_onehot, y_prompt, y_sample):
    ctx = ExitStack()
    with ctx:
        def sb(name, cols, parts=P, dt=F32):
            return ctx.enter_context(nc.sbuf_tensor(name, [parts, cols], dt))

        def sem(name):
            return ctx.enter_context(nc.semaphore(name))

        SLOT = KD * HF
        slot_gate = sb("slot_gate", SLOT)
        slot_up = sb("slot_up", SLOT)
        slot_down = sb("slot_down", FT * D)
        ring = sb("ring", 2 * KD * 512)
        x = sb("x", NT * D)
        cst = sb("cst", C_W)
        small = sb("small", 400)
        xv = x[:, :].rearrange("p (t d) -> p t d", t=NT)

        qT = slot_gate[:, 0:3072].rearrange("p (c n) -> p c n", c=4)
        kT = slot_gate[:, 3072:6144].rearrange("p (c n) -> p c n", c=4)
        vv = slot_gate[:, 6144:9216].rearrange("p (t n) -> p t n", t=NT)
        sq = slot_gate[:, 9216:10240].rearrange("p (b n) -> p b n", b=2)
        qn = slot_gate[:, 10240:11264].rearrange("p (b n) -> p b n", b=2)
        hn = slot_gate[:, 0:2048].rearrange("p (b n) -> p b n", b=2)
        junk = slot_gate[:, 2048:3072]
        g1b = slot_gate[:, 3072:4096]
        hT = slot_up[:, 0:6144].rearrange("p (k n) -> p k n", k=KD)
        ydT = slot_up[:, 6144:9216].rearrange("p (c n) -> p c n", c=4)
        bias = slot_up[:, 9216:9216 + 2 * BW].rearrange("p (b n) -> p b n", b=2)
        mT = slot_down[:, 0:6144].rearrange("p (k n) -> p k n", k=KD)
        ynT = slot_down[:, 6144:9216].rearrange("p (c n) -> p c n", c=4)
        y_tok = slot_down[:, 0:3072].rearrange("p (t n) -> p t n", t=NT)
        sT = slot_down[:, 3072:6144].rearrange("p (b m n) -> p b m n", b=3, m=2)
        aT = slot_down[:, 9216:10240].rearrange("p (b n) -> p b n", b=2)
        gtmp = slot_down[:, 9216:10752].rearrange("p (b n) -> p b n", b=4)
        wr = ring[:, :].rearrange("p (b n) -> p b n", b=2)
        xe = ring[0:CAP, 0:1024]
        xeT = ring[:, 1024:1792].rearrange("p (k s) -> p k s", k=KD)
        hg = ring[:, 1792:2848].rearrange("p (f s) -> p f s", f=FT)
        hT2 = ring[:, 2848:3904].rearrange("p (f s) -> p f s", f=FT)
        yT = ring[:, 3904:4672].rearrange("p (k s) -> p k s", k=KD)
        ye = ring[0:CAP, 4672:5696]
        scat = ring[0:CAP, 5696:6464]
        iota_tok = ring[0:CAP, 6464:7232]
        tn = slot_down[:, 6144:8192].rearrange("p (b n) -> p b n", b=2)
        tT = slot_down[:, 8192:10240].rearrange("p (b k n) -> p b k n", b=2, k=KD)
        g2b = slot_down[:, 10240:11264]
        wrt = sb("wrt", KD * E)
        wrt_v = wrt[:, :].rearrange("p (k e) -> p k e", k=KD)
        affT = slot_down[0:E, 0:768]
        work = slot_down[0:E, 768:1536]
        selT = slot_down[0:E, 1536:2304]
        cumT = slot_down[0:E, 2304:3072]
        ones = slot_down[0:E, 3072:3584]
        G = slot_down[:, 3584:5632].rearrange("p (b e s) -> p b e s", b=2, e=E)
        rk = slot_down[:, 5632:5728].rearrange("p (t e) -> p t e", t=NT)
        aff = small[:, 200:296].rearrange("p (t e) -> p t e", t=NT)
        R = slot_down[:, 5760:5952].rearrange("p (t e c) -> p t e c", t=NT, c=2)
        idxf = sb("idxf", 17, CAP)
        gate_s = sb("gate_s", 17, CAP)
        idxi = sb("idxi", 17, CAP, I32)
        cur_i = sb("cur_i", 1, CAP, I32)
        cur_f = sb("cur_f", 1, CAP)
        cur_g = sb("cur_g", 1, CAP)
        napad = slot_down[0:120, 6144:6272]
        t5h = slot_down[0:32, 6272:7296]
        t5b = slot_down[0:4, 7296:8320]
        t5t = slot_down[0:32, 8320:8324]
        lamv = slot_down[:, 8448:8704].rearrange("p (v d) -> p v d", v=4)
        lamj = slot_down[:, 8704:8768]

        ident = cst[:, C_ID:C_ID + 128]
        mask = cst[:, C_MASK:C_MASK + 64]
        tokid = cst[:, C_TOK:C_TOK + NT]
        slot1 = cst[:, C_SLOT:C_SLOT + 64]
        mhalf = cst[:, C_POW:C_POW + 64]

        ss = small[:, 0:32].rearrange("p (b n) -> p b n", b=4)
        rs = small[:, 32:64].rearrange("p (b n) -> p b n", b=4)
        nss = small[:, 64:70]
        nrs = small[:, 72:78]
        mx = small[:, 80:86].rearrange("p (b m) -> p b m", b=3)
        sm = small[:, 88:94].rearrange("p (b m) -> p b m", b=3)
        ri = small[:, 96:104].rearrange("p (b m) -> p b m", b=4)
        lam = small[:, 104:108]
        gains = small[:, 112:120]
        m8 = small[0:E, 120:128]
        rmx = small[:, 128:134]
        rsm = small[:, 136:142]
        rrs = small[:, 144:150]
        mx_raw = small[:, 160:166].rearrange("p (b m) -> p b m", b=3)

        PS = ctx.enter_context(nc.psum_tensor("PS", [P, 8, 512], F32))
        t5_dram = nc.dram_tensor("t5_dram", [4, 1024], F32, kind="Internal").ap()
        na_dram = nc.dram_tensor("na_dram", [120, 128], F32, kind="Internal").ap()
        t5_rep = nc.dram_tensor("t5_rep", [4, P, 1024], F32, kind="Internal").ap()
        na_rep = nc.dram_tensor("na_rep", [8, 64, NA_ROWS * 128], F32, kind="Internal").ap()
        t_dram = nc.dram_tensor("t_dram", [N, D], F32, kind="Internal").ap()

        s_x = [sem(f"x_loaded{t}") for t in range(NT)]
        s_cst = sem("constants_loaded")
        s_lamv = sem("lambdas_loaded")
        s_tab = sem("tables_loaded")
        s_wr = [sem(f"ring_loaded{b}") for b in range(2)]
        s_nz = sem("na_pad_zeroed")
        s_nt = sem("na_table_in_pad")
        s_tm = sem("t5_rows_ready")
        s_tc = sem("t5_rows_in_sbuf")
        s_scr = sem("bias_rows_in_dram")
        s_rep = sem("bias_rows_replicated")
        s_b = [sem(f"bias_loaded{b}") for b in range(2)]
        s_bm = sem("bias_masked")
        s_pha = sem("act_done_with_stage")
        s_phd = sem("dve_done_with_stage")
        s_dv = sem("dve_chain")
        s_ac = sem("act_chain")
        s_pl = sem("pool_chain")
        s_lam = sem("lambda_sums_ready")
        s_lae = sem("lambda_exps_ready")

        chain_counts = {"dve": 0, "act": 0, "pool": 0}

        def linker(eng, s, key):
            def link(ins):
                chain_counts[key] += 1
                ins.then_inc(s, 1)
                eng.wait_ge(s, chain_counts[key])
            return link

        sems = {}

        def S(stage, name):
            k = f"{stage}_{name}"
            if k not in sems:
                sems[k] = sem(k)
            return sems[k]

        W_TOK = w_in.rearrange("(k p) c -> p k c", p=P)
        WBD = w_branch_diff.rearrange("(k p) c -> p k c", p=P)
        WBN = w_branch_na.rearrange("(k p) c -> p k c", p=P)
        WO = w_out.rearrange("(k p) c -> p k c", p=P)
        GD0 = 6 * HW

        def xsrc(a, b, t):
            return a[t * P:(t + 1) * P, :] if t < 2 else b[(t - 2) * P:(t - 1) * P, :]

        def items(heads):
            return [(h, qt, t0, nt) for h in range(heads) for (t0, nt) in GROUPS for qt in range(nt)]

        DI, NI = items(4), items(8)
        ATT = {"diff": DI, "na": NI}
        HPI = NT

        def stage_done(eng, k):
            eng.wait_ge(s_pha, k)
            eng.wait_ge(s_phd, k)

        block = ctx.enter_context(nc.Block())

        @block.sync
        def _(sp):
            for t in range(NT):
                sp.dma_start(xv[:, t, :], xsrc(x_prompt, x_sample, t)).then_inc(s_x[t], 16)
            n = 0

            def ring_wait():
                u = n - 2
                if 0 <= u < 3:
                    sp.wait_ge(S("pd", "p"), 6 * (u + 1))
                elif 3 <= u < 6:
                    sp.wait_ge(S("pn", "p"), 6 * (u - 2))
                elif u >= 6:
                    sp.wait_ge(S("g", "prod"), 8 * (u - 5))

            for c in range(6):
                ring_wait()
                dst = wr[:, n % 2, :].rearrange("p (k c) -> p k c", k=KD)
                sp.dma_start(dst, W_TOK[:, :, c * HW:(c + 1) * HW]).then_inc(s_wr[n % 2], 16)
                n += 1
            for j in range(KD):
                ring_wait()
                base = wr[:, n % 2, :]
                for q, (src, kt, c0) in enumerate(((W_TOK, 8, GD0 + j * P), (W_TOK, 8, GD0 + D + j * P),
                                                   (WBD, 4, j * P), (WBN, 4, j * P))):
                    o = (0, 1024, 2048, 2560)[q]
                    sp.dma_start(base[:, o:o + kt * P].rearrange("p (k c) -> p k c", k=kt),
                                 src[:, :, c0:c0 + P]).then_inc(s_wr[n % 2], 16)
                n += 1
            for c in range(2):
                ring_wait()
                dst = wr[:, n % 2, :].rearrange("p (k c) -> p k c", k=KD)
                sp.dma_start(dst, WO[:, :, c * 512:(c + 1) * 512]).then_inc(s_wr[n % 2], 16)
                n += 1
                if c == 0:
                    stage_done(sp, 7)
            g_src = w_expert_gate.rearrange("e (k p) f -> e p k f", p=P)
            u_src = w_expert_up.rearrange("e (k p) f -> e p k f", p=P)
            d_src = w_expert_down.rearrange("e (h f p) d -> e h p f d", p=P, h=2)
            sg_, su_, sd_ = S("x", "gate_w"), S("x", "up_w"), S("x", "down_w")
            gv = slot_gate[:, :].rearrange("p (k f) -> p k f", k=KD)
            uv = slot_up[:, :].rearrange("p (k f) -> p k f", k=KD)
            dv = slot_down[:, :].rearrange("p (f d) -> p f d", f=FT)
            with sp.Fori(0, E) as e:
                for h in range(2):
                    sp.wait_ge(S("x", "gate_group"), e * 6 + 3 * h + 1)
                    sp.dma_start(gv, g_src[e, :, :, h * HF:(h + 1) * HF]).then_inc(sg_, 16)
                    if h == 0:
                        stage_done(sp, 8)
                    sp.wait_ge(S("x", "up_group"), e * 6 + 3 * h + 1)
                    sp.dma_start(uv, u_src[e, :, :, h * HF:(h + 1) * HF]).then_inc(su_, 16)
                    if h == 0:
                        sp.wait_ge(S("rt", "tables_done"), 1)
                        sp.wait_ge(S("n2", "stored0"), 48)
                        sp.wait_ge(S("n2", "stored1"), 48)
                    sp.wait_ge(S("x", "down_bank"), e * 4 + 2 * h + 1)
                    sp.dma_start(dv, d_src[e, h, :, :, :]).then_inc(sd_, 16)
            sp.wait_ge(S("x", "added"), 12 * E + 1)
            for t in range(NT):
                sp.dma_start(xsrc(y_prompt, y_sample, t), xv[:, t, :]).then_inc(S("x", "stored"), 16)
            sp.wait_ge(S("x", "stored"), 16 * NT)

        @block.gpsimd
        def _(pool):
            link = linker(pool, s_pl, "pool")
            pool.dma_start(cst[:, :], consts).then_inc(s_cst, 16)
            pool.dma_start(g1b, norm1_g.to_broadcast((P, D))).then_inc(s_cst, 16)
            nc.gpsimd.memset(napad, 0.0).then_inc(s_nz, 1)
            for i, v in enumerate((lambda_q1, lambda_k1, lambda_q2, lambda_k2)):
                pool.dma_start(lamv[:, i, :], v.to_broadcast((P, 64))).then_inc(s_lamv, 16)
            for col, g, w in ((0, diff_q_norm, 64), (1, diff_k_norm, 64), (2, diff_subln_g, 128), (3, na_q_norm, 64),
                              (4, na_k_norm, 64)):
                for r in range(P // w):
                    pool.dma_start(gains[r * w:(r + 1) * w, col:col + 1],
                                   g.rearrange("a d -> d a")).then_inc(s_lamv, 16)
            pool.dma_start(t5h, t5_onehot).then_inc(s_tab, 16)
            pool.dma_start(t5t, rel_bias).then_inc(s_tab, 16)
            pool.wait_ge(s_nz, 1)
            pool.dma_start(napad[:, 48:79], na_rpb.rearrange("h r c -> (h r) c")).then_inc(s_nt, 16)
            pool.wait_ge(s_nt, 16)
            pool.dma_start(na_dram, napad).then_inc(s_scr, 16)
            pool.wait_ge(s_tc, 1)
            pool.dma_start(t5_dram, t5b).then_inc(s_scr, 16)
            pool.wait_ge(s_scr, 32)
            t5_src = bass.AP(t5_dram.tensor, 0, [[1024, 4], [0, P], [1, 1024]])
            na_src = bass.AP(na_dram.tensor, 0, [[NA_ROWS * 128, 8], [0, 64], [1, NA_ROWS * 128]])
            pool.dma_start(t5_rep, t5_src).then_inc(s_rep, 16)
            pool.dma_start(na_rep, na_src).then_inc(s_rep, 16)
            pool.dma_start(wrt_v, w_router.rearrange("(k p) e -> p k e", p=P)).then_inc(S("rt", "wrt"), 16)
            pool.wait_ge(s_cst, 32)

            def rsqrt(out, in_, w, wait, val, done):
                pool.wait_ge(wait, val)
                nc.gpsimd.tensor_tensor(out, in_, mhalf[:, 0:w], ALU.pow).then_inc(done, 1)

            for t in range(NT):
                rsqrt(nrs[:, t:t + 1], nss[:, t:t + 1], 1, S("n1", "ss"), t + 1, S("n1", "rs"))

            def load_bias(nh):
                b = nh % 2
                if nh == 0:
                    pool.wait_ge(s_rep, 32)
                if nh >= 2:
                    br, used = ("diff", nh - 1) if nh - 2 < 4 else ("na", nh - 5)
                    pool.wait_ge(S(br, "biased"), HPI * used)
                if nh < 4:
                    src = bass.AP(t5_rep.tensor, nh * P * 1024 + 127, [[1023, 128], [1, BW]])
                    pool.dma_start(bias[:, b, :], src).then_inc(s_b[b], 16)
                else:
                    h = nh - 4
                    for rr in range(2):
                        src = bass.AP(na_rep.tensor, (h * 64 * NA_ROWS + 1 - rr) * 128 + 63,
                                      [[NA_ROWS * 128 - 1, 64], [128, 14], [1, 64]])
                        pool.dma_start(bias[64 * rr:64 * rr + 64, b, :].rearrange("p (j k) -> p j k", j=14),
                                       src).then_inc(s_b[b], 16)

            def mask_bias(nh):
                b = nh % 2
                pool.wait_ge(s_b[b], 32 * (nh // 2 - 2) + 64 if nh >= 4 else 0)
                v = bias[:, b, :].rearrange("p (j k) -> p j k", j=14)
                nc.gpsimd.tensor_tensor(v, v, mask.unsqueeze(1).to_broadcast((P, 14, 64)), ALU.add).then_inc(s_bm, 1)

            def norm_rs(stage, jobs, w):
                for j in range(jobs):
                    rsqrt(rs[:, j % 4, 0:w], ss[:, j % 4, 0:w], w, S(stage, "ss"), j + 1, S(stage, "rs"))

            load_bias(0)
            load_bias(1)
            norm_rs("pd", 12, 8)
            load_bias(2)
            load_bias(3)
            load_bias(4)
            mask_bias(4)
            load_bias(5)
            mask_bias(5)
            norm_rs("yd", NT, 4)
            norm_rs("pn", 12, 8)
            for nh in range(6, 12):
                load_bias(nh)
                mask_bias(nh)
            stage_done(pool, 8)
            pool.dma_start(g2b, norm2_g.to_broadcast((P, D))).then_inc(S("rt", "g2"), 16)
            for t in range(NT):
                rsqrt(nrs[:, t:t + 1], nss[:, t:t + 1], 1, S("n2", "ss"), t + 1, S("n2", "rs"))
                pool.wait_ge(S("n2", "hn"), t + 1)
                pool.dma_start(t_dram[t * P:(t + 1) * P, :], tn[:, t % 2, :]).then_inc(S("n2", f"stored{t % 2}"), 16)
            stage_done(pool, 10)
            nc.gpsimd.iota(iota_tok, pattern=[[1, N]], base=0, channel_multiplier=0,
                           allow_small_or_imprecise_dtypes=True).then_inc(S("x", "iota"), 1)
            pool.wait_ge(S("n2", "stored0"), 48)
            pool.wait_ge(S("n2", "stored1"), 48)

            def gather():
                pool.indirect_dma_start(xe, None, t_dram, bass.IndirectOffsetOnAxis(ap=cur_i[:, 0:1], axis=0)
                                        ).then_inc(S("x", "xe"), 16)

            pool.wait_ge(S("x", "cur"), 1)
            gather()
            for e in range(E):
                pool.wait_ge(S("x", "cur"), e + 2)
                pool.wait_ge(S("x", "xe_t"), 2 * e + 2)
                gather()

        @block.tensor
        def _(pe):
            mm = nc.tensor.matmul
            pe.sem_inc(S("x", "gate_group"), 1)
            pe.sem_inc(S("x", "up_group"), 1)
            pe.sem_inc(S("x", "down_bank"), 1)
            pe.sem_inc(S("x", "scattered"), 1)
            pe.wait_ge(s_cst, 32)
            pe.wait_ge(s_tab, 32)
            for b in range(2):
                i = mm(PS[0:4, 6 + b, :], t5t, t5h[:, b * 512:(b + 1) * 512], start=True, stop=True)
            i.then_inc(s_tm, 1)
            for t in range(NT):
                pe.wait_ge(S("n1", "hn"), t + 1)
                for q in range(2):
                    j = 2 * t + q
                    if j >= 4:
                        pe.wait_ge(S("n1", "tev"), j - 3)
                    for k in range(4):
                        i = nc.tensor.transpose(PS[:, j % 4, k * P:(k + 1) * P],
                                                hn[:, t % 2, (4 * q + k) * P:(4 * q + k + 1) * P], ident)
                    i.then_inc(S("n1", "tr"), 1)
            chunk = 0

            def transposes(stage, jt, src):
                if jt >= 2:
                    pe.wait_ge(S(stage, "tev"), jt - 1)
                for c in range(4):
                    i = nc.tensor.transpose(PS[:, 4 + jt % 2, c * P:(c + 1) * P], src[:, c * P:(c + 1) * P], ident)
                i.then_inc(S(stage, "tr"), 1)

            def project(stage, k, chunk):
                stage_done(pe, k)
                for j in range(18 + 2):
                    if j < 18:
                        c, t = divmod(j, NT)
                        n = chunk + c
                        if t == 0:
                            pe.wait_ge(s_wr[n % 2], 16 * (n // 2 + 1))
                        if j >= 4:
                            pe.wait_ge(S(stage, "pused"), j - 3)
                        w = wr[:, n % 2, :].rearrange("p (k c) -> p k c", k=KD)
                        for k_ in range(KD):
                            i = mm(PS[:, j % 4, :], hT[:, k_, t * P:(t + 1) * P], w[:, k_, :],
                                   start=k_ == 0, stop=k_ == KD - 1)
                        i.then_inc(S(stage, "p"), 1)
                    jt = j - 2
                    if 0 <= jt < 12:
                        pe.wait_ge(S(stage, "qn"), jt + 1)
                        transposes(stage, jt, qn[:, jt % 2, :])

            def attend(br, k):
                stage_done(pe, k)
                L = ATT[br]
                nm = 2 if br == "diff" else 1
                for step in range(len(L) + 3):
                    if step < len(L):
                        h, qt, t0, nt = L[step]
                        if step >= 2:
                            pe.wait_ge(S(br, "biased"), step - 1)
                        for m in range(nm):
                            c, r = (h, m) if br == "diff" else (h // 2, h % 2)
                            i = mm(PS[:, 2 * (step % 2) + m, 0:nt * P],
                                   qT[64 * r:64 * r + 64, c, (t0 + qt) * P:(t0 + qt + 1) * P],
                                   kT[64 * r:64 * r + 64, c, t0 * P:(t0 + nt) * P], start=True, stop=True)
                        i.then_inc(S(br, "log"), 1)
                    a = step - 2
                    if 0 <= a < len(L):
                        h, qt, t0, nt = L[a]
                        pe.wait_ge(S(br, "probs"), a + 1)
                        if a >= 2:
                            pe.wait_ge(S(br, "aT"), a - 1)
                        for c in range(nt):
                            i = nc.tensor.transpose(PS[:, 4 + a % 2, c * P:(c + 1) * P],
                                                    sT[:, a % 3, 0, c * P:(c + 1) * P], ident)
                        i.then_inc(S(br, "tr"), 1)
                    a = step - 3
                    if 0 <= a < len(L):
                        h, qt, t0, nt = L[a]
                        pe.wait_ge(S(br, "aT"), a + 1)
                        if a >= 2:
                            pe.wait_ge(S(br, "out"), a - 1)
                        w = P if br == "diff" else 64
                        for c in range(nt):
                            i = mm(PS[:, 6 + a % 2, 0:w], aT[:, a % 2, c * P:(c + 1) * P],
                                   vv[:, t0 + c, h * w:(h + 1) * w], start=c == 0, stop=c == nt - 1)
                        i.then_inc(S(br, "pv"), 1)

            project("pd", 1, 0)
            attend("diff", 2)
            stage_done(pe, 3)
            for t in range(NT):
                pe.wait_ge(S("yd", "qn"), t + 1)
                transposes("yd", t, qn[:, t % 2, :])
            project("pn", 4, 3)
            attend("na", 5)
            stage_done(pe, 6)
            for t in range(NT):
                transposes("yn", t, y_tok[:, t, :])
            stage_done(pe, 7)
            for j in range(KD):
                n = 6 + j
                need = 48 + 64 * (j // 2 + 1)
                pe.wait_ge(s_wr[n % 2], need)
                base = wr[:, n % 2, :]
                for hf in range(2):
                    s = 2 * j + hf
                    if s >= 2:
                        pe.wait_ge(S("g", "merged"), s - 1)
                    cols = slice(hf * 384, hf * 384 + 384)
                    for q, (o, kt, src) in enumerate(((0, 8, hT), (1024, 8, hT), (2048, 4, ydT), (2560, 4, ynT))):
                        for k in range(kt):
                            i = mm(PS[:, 4 * (s % 2) + q, 0:384], base[:, o + k * P:o + (k + 1) * P],
                                   src[:, k, cols], start=k == 0, stop=k == kt - 1)
                        i.then_inc(S("g", "prod"), 1)
            stage_done(pe, 8)
            for c in range(2):
                n = 14 + c
                pe.wait_ge(s_wr[n % 2], 48 + 256 + 16)
                w = wr[:, n % 2, :].rearrange("p (k c) -> p k c", k=KD)
                for t in range(NT):
                    j = c * NT + t
                    if j >= 8:
                        pe.wait_ge(S("o", "added"), j - 7)
                    for k in range(KD):
                        i = mm(PS[:, j % 8, :], mT[:, k, t * P:(t + 1) * P], w[:, k, :], start=k == 0,
                               stop=k == KD - 1)
                    i.then_inc(S("o", "prod"), 1)
            stage_done(pe, 9)
            pe.wait_ge(S("rt", "wrt"), 16)
            for t in range(NT):
                pe.wait_ge(S("n2", "hn"), t + 1)
                for q in range(2):
                    j = 2 * t + q
                    if j >= 4:
                        pe.wait_ge(S("n2", "tev"), j - 3)
                    for k in range(4):
                        i = nc.tensor.transpose(PS[:, j % 4, k * P:(k + 1) * P],
                                                tn[:, t % 2, (4 * q + k) * P:(4 * q + k + 1) * P], ident)
                    i.then_inc(S("n2", "tr"), 1)
                pe.wait_ge(S("n2", "tev"), 2 * t + 2)
                for k in range(KD):
                    i = mm(PS[:, 4, t * E:(t + 1) * E], tT[:, t % 2, k, :], wrt_v[:, k, :],
                           start=k == 0, stop=k == KD - 1)
                i.then_inc(S("rt", "logits"), 1)
            pe.wait_ge(S("rt", "aff"), 1)
            for t in range(NT):
                i = nc.tensor.transpose(PS[0:E, 5 + t // 4, (t % 4) * P:(t % 4 + 1) * P], aff[:, t, :], ident)
            i.then_inc(S("rt", "affT"), 1)
            pe.wait_ge(S("rt", "rank"), 1)
            for t in range(NT):
                i = nc.tensor.transpose(PS[:, 7, t * E:(t + 1) * E], cumT[:, t * P:(t + 1) * P], ident[0:E, 0:E])
            i.then_inc(S("rt", "rkT"), 1)
            for t in range(NT):
                pe.wait_ge(S("rt", "G"), t + 1)
                smp = t >= 2
                w, p0 = (CS, 0) if smp else (CP, CS)
                first = 2 if smp else 0
                last = NT - 1 if smp else 1
                for e in range(E):
                    i = mm(PS[p0:p0 + w, 1 if smp else 0, 2 * e:2 * e + 2], G[:, t % 2, e, 0:w], R[:, t, e, :],
                           start=(t == first and e == 0), stop=t == last, skip_group_check=True)
                i.then_inc(S("rt", "slots"), 1)

            gv = slot_gate[:, :].rearrange("p (k f) -> p k f", k=KD)
            uv = slot_up[:, :].rearrange("p (k f) -> p k f", k=KD)
            dv = slot_down[:, :].rearrange("p (f d) -> p f d", f=FT)
            TILES = [range(0, 4), range(4, 8), range(8, FT)]

            def gather_t():
                for q in range(2):
                    for k in range(4):
                        i = nc.tensor.transpose(PS[:, 5 + q, k * CAP:(k + 1) * CAP],
                                                xe[:, (4 * q + k) * P:(4 * q + k + 1) * P], ident[0:CAP, 0:CAP])
                    i.then_inc(S("x", "xe_t"), 1)

            stage_done(pe, 10)
            pe.wait_ge(S("x", "xe"), 16)
            gather_t()
            with pe.Fori(0, E) as e:
                for h in range(2):
                    pe.wait_ge(S("x", "gate_w"), e * 32 + 16 * (h + 1))
                    if h == 0:
                        pe.wait_ge(S("x", "xeT"), e * 2 + 2)
                    pe.wait_ge(S("x", "hidden"), e * 6 + 3 * h + 1)
                    for g, tiles in enumerate(TILES):
                        for u, f in enumerate(tiles):
                            for k in range(KD):
                                i = mm(PS[:, g, u * CAP:(u + 1) * CAP], gv[:, k, f * P:(f + 1) * P], xeT[:, k, :],
                                       start=k == 0, stop=k == KD - 1)
                        i.then_inc(S("x", "gate_group"), 1)
                    pe.wait_ge(S("x", "up_w"), e * 32 + 16 * (h + 1))
                    for g, tiles in enumerate(TILES):
                        pe.wait_ge(S("x", "silu"), e * 6 + 3 * h + g + 1)
                        for u, f in enumerate(tiles):
                            for k in range(KD):
                                i = mm(PS[:, g, u * CAP:(u + 1) * CAP], uv[:, k, f * P:(f + 1) * P], xeT[:, k, :],
                                       start=k == 0, stop=k == KD - 1)
                        i.then_inc(S("x", "up_group"), 1)
                    if h == 1:
                        pe.wait_ge(S("x", "xe"), e * 16 + 32)
                        pe.wait_ge(S("x", "added"), e * 12 + 1)
                        gather_t()
                    pe.wait_ge(S("x", "down_w"), e * 32 + 16 * (h + 1))
                    pe.wait_ge(S("x", "hidden"), e * 6 + 3 * h + 3 + 1)
                    if h == 0:
                        pe.wait_ge(S("x", "yT0"), e + 1)
                        pe.wait_ge(S("x", "yT1"), e + 1)
                    for b in range(2):
                        for d in range(4):
                            for f in range(FT):
                                i = mm(PS[:, 3 + b, d * CAP:(d + 1) * CAP],
                                       dv[:, f, (4 * b + d) * P:(4 * b + d + 1) * P], hT2[:, f, :],
                                       start=(h == 0 and d == 0 and f == 0), stop=(h == 1 and f == FT - 1),
                                       skip_group_check=True)
                        i.then_inc(S("x", "down_bank"), 1)
                for b in range(2):
                    pe.wait_ge(S("x", f"yT{b}"), e + 1 + 1)
                    pe.wait_ge(S("x", "xeT"), e * 2 + 4)
                    for d in range(4):
                        i = nc.tensor.transpose(PS[0:CAP, 5 + b, d * P:(d + 1) * P], yT[:, 4 * b + d, :], ident)
                    i.then_inc(S("x", "y_t"), 1)
                pe.wait_ge(S("x", "ye"), e * 2 + 2)
                pe.wait_ge(S("x", "onehot"), e + 1)
                for j in range(12):
                    t, half = divmod(j, 2)
                    if j >= 3:
                        pe.wait_ge(S("x", "added"), e * 12 + j - 2 + 1)
                    mm(PS[:, 5 + j % 3, :], scat[:, t * P:(t + 1) * P], ye[:, half * 512:(half + 1) * 512],
                       start=True, stop=True).then_inc(S("x", "scattered"), 1)

        @block.scalar
        def _(act):
            a_ = nc.scalar.activation
            act.sem_inc(S("x", "yT0"), 1)
            link = linker(act, s_ac, "act")
            act.wait_ge(s_tm, 1)
            a_(t5b, PS[0:4, 6:8, :].rearrange("p b n -> p (b n)"), ACT.Copy).then_inc(s_tc, 1)
            act.wait_ge(s_lam, 1)
            a_(lam[:, 2:4], lam[:, 0:2], ACT.Exp).then_inc(s_lae, 1)
            for t in range(NT + 1):
                if t < NT:
                    act.wait_ge(s_x[t], 16)
                    if t > 0:
                        act.wait_ge(S("n1", "sq"), t)
                    a_(junk, xv[:, t, :], ACT.Square, accum_out=nss[:, t:t + 1]).then_inc(S("n1", "sq"), 1)
                if t > 0:
                    for q in range(2):
                        j = 2 * (t - 1) + q
                        act.wait_ge(S("n1", "tr"), j + 1)
                        a_(hT[:, 4 * q:4 * q + 4, (t - 1) * P:t * P],
                           PS[:, j % 4, :].rearrange("p (k n) -> p k n", k=4), ACT.Copy).then_inc(S("n1", "tev"), 1)
            act.wait_ge(S("n1", "tev"), 2 * NT)
            act.sem_inc(s_pha, 1)

            def evac_t(stage, jt, dst, gain):
                act.wait_ge(S(stage, "tr"), jt + 1)
                src = PS[:, 4 + jt % 2, :].rearrange("p (c n) -> p c n", c=4)
                if gain is None:
                    i = a_(dst, src, ACT.Copy)
                else:
                    i = a_(dst, src, ACT.Copy, scale=gains[:, gain:gain + 1])
                i.then_inc(S(stage, "tev"), 1)

            def square(stage, j, src):
                if j >= 2:
                    act.wait_ge(S(stage, "ss"), j - 1)
                a_(sq[:, j % 2, :], src, ACT.Square).then_inc(S(stage, "sq"), 1)

            def project(stage, g0):
                for j in range(14):
                    if j < 12:
                        act.wait_ge(S(stage, "p"), j + 1)
                        square(stage, j, PS[:, j % 4, :])
                    jt = j - 2
                    if jt >= 0:
                        c, t = divmod(jt, NT)
                        evac_t(stage, jt, (qT, kT)[c][:, :, t * P:(t + 1) * P], g0 + c)
                act.wait_ge(S(stage, "tev"), 12)
                act.sem_inc(s_pha, 1)

            def attend(br):
                L = ATT[br]
                nm = 2 if br == "diff" else 1
                for step in range(len(L) + 2):
                    if step < len(L):
                        n = L[step][3] * P
                        act.wait_ge(S(br, "max"), step + 1)
                        for m in range(nm):
                            v = sT[:, step % 3, m, 0:n]
                            i = a_(v, v, ACT.Exp, bias=mx[:, step % 3, m:m + 1], accum_out=sm[:, step % 3, m:m + 1])
                        i.then_inc(S(br, "exp"), 1)
                    a = step - 2
                    if a >= 0:
                        n = L[a][3] * P
                        act.wait_ge(S(br, "tr"), a + 1)
                        if a >= 2:
                            act.wait_ge(S(br, "pv"), a - 1)
                        a_(aT[:, a % 2, 0:n], PS[:, 4 + a % 2, 0:n], ACT.Copy).then_inc(S(br, "aT"), 1)
                act.wait_ge(S(br, "aT"), len(L))
                act.sem_inc(s_pha, 1)

            project("pd", 0)
            attend("diff")
            for t in range(NT + 1):
                if t < NT:
                    if t == 0:
                        act.wait_ge(S("diff", "out"), len(DI))
                    square("yd", t, y_tok[:, t, :])
                if t > 0:
                    evac_t("yd", t - 1, ydT[:, :, (t - 1) * P:t * P], 2)
            act.wait_ge(S("yd", "tev"), NT)
            act.sem_inc(s_pha, 1)
            project("pn", 3)
            attend("na")
            for t in range(NT):
                evac_t("yn", t, ynT[:, :, t * P:(t + 1) * P], None)
            act.wait_ge(S("yn", "tev"), NT)
            act.sem_inc(s_pha, 1)
            for s in range(16):
                if s >= 2:
                    act.wait_ge(S("g", "merged"), s - 1)
                for q in range(2):
                    act.wait_ge(S("g", "prod"), 4 * s + q + 1)
                    a_(gtmp[:, 2 * (s % 2) + q, :], PS[:, 4 * (s % 2) + q, 0:384], ACT.Sigmoid).then_inc(S("g", "sig"), 1)
            act.wait_ge(S("g", "sig"), 32)
            act.sem_inc(s_pha, 1)
            act.sem_inc(s_pha, 1)
            for t in range(NT):
                act.wait_ge(S("o", "added"), NT + t + 1)
                if t > 0:
                    act.wait_ge(S("n2", "sq"), t)
                else:
                    act.wait_ge(S("rt", "g2"), 16)
                a_(ring[:, 0:1024], xv[:, t, :], ACT.Square, accum_out=nss[:, t:t + 1]).then_inc(S("n2", "sq"), 1)
            for t in range(NT):
                for q in range(2):
                    j = 2 * t + q
                    act.wait_ge(S("n2", "tr"), j + 1)
                    if t >= 2:
                        act.wait_ge(S("rt", "logits"), t - 1)
                    a_(tT[:, t % 2, 4 * q:4 * q + 4, :], PS[:, j % 4, :].rearrange("p (k n) -> p k n", k=4),
                       ACT.Copy).then_inc(S("n2", "tev"), 1)
            act.wait_ge(S("rt", "shift"), 1)
            for t in range(NT):
                i = a_(aff[:, t, :], aff[:, t, :], ACT.Exp, bias=rmx[:, t:t + 1], accum_out=rsm[:, t:t + 1])
            i.then_inc(S("rt", "exp"), 1)
            act.wait_ge(S("rt", "exp"), 1)
            act.sem_inc(s_pha, 1)
            TILES = [(0, 4), (4, 4), (8, FT - 8)]
            def xeT_evac(n):
                act.wait_ge(S("x", "xe_t"), n)
                a_(xeT[:, 0:4, :], PS[:, 5, 0:4 * CAP].rearrange("p (k s) -> p k s", k=4), ACT.Copy
                   ).then_inc(S("x", "xeT"), 1)

            xeT_evac(1)
            with act.Fori(0, E) as e:
                for h in range(2):
                    for g, (f0, nf) in enumerate(TILES):
                        act.wait_ge(S("x", "gate_group"), e * 6 + 3 * h + g + 1 + 1)
                        a_(hg[:, f0:f0 + nf, :], PS[:, g, 0:nf * CAP].rearrange("p (f s) -> p f s", f=nf), ACT.Silu
                           ).then_inc(S("x", "silu"), 1)
                xeT_evac(e * 2 + 3)
                act.wait_ge(S("x", "down_bank"), e * 4 + 3 + 1)
                a_(yT[:, 0:4, :], PS[:, 3, 0:4 * CAP].rearrange("p (k s) -> p k s", k=4), ACT.Copy
                   ).then_inc(S("x", "yT0"), 1)
                act.wait_ge(S("x", "y_t"), e * 2 + 1)
                act.wait_ge(S("x", "onehot"), e + 1)
                a_(ye[:, 0:512], PS[0:CAP, 5, :], ACT.Copy, scale=cur_g[:, 0:1]).then_inc(S("x", "ye"), 1)

        @block.vector
        def _(dve):
            v = nc.vector
            dve.sem_inc(S("x", "hidden"), 1)
            dve.sem_inc(S("x", "yT1"), 1)
            dve.sem_inc(S("x", "added"), 1)
            link = linker(dve, s_dv, "dve")
            dve.wait_ge(s_lamv, 16 * 13)
            for m in range(2):
                i = v.tensor_tensor(lamv[:, 2 * m, :], lamv[:, 2 * m, :], lamv[:, 2 * m + 1, :], ALU.mult)
            link(i)
            for m in range(2):
                i = v.tensor_reduce(lam[:, m:m + 1], lamv[:, 2 * m, :], AX.X, ALU.add)
            i.then_inc(s_lam, 1)
            dve.wait_ge(s_lam, 1)
            for c, s_ in ((0, 0.125), (2, 1.0 - LAM0), (3, 0.125)):
                i = v.tensor_scalar(gains[:, c:c + 1], gains[:, c:c + 1], s_, None, ALU.mult)
            dve.wait_ge(s_lae, 1)
            i = v.scalar_tensor_tensor(lam[:, 0:1], lam[:, 2:3], LAM0, lam[:, 3:4], ALU.add, ALU.subtract)
            link(i)
            dve.wait_ge(s_cst, 32)

            def mean_eps(out, in_, w, done):
                return v.tensor_scalar(out, in_, 1.0 / w, EPS, ALU.mult, ALU.add).then_inc(done, 1)

            def norm_tokens(stage, gb, dst, bufs_free):
                for t in range(NT + 1):
                    if t < NT:
                        dve.wait_ge(S(stage, "sq"), t + 1)
                        mean_eps(nss[:, t:t + 1], nss[:, t:t + 1], D, S(stage, "ss"))
                    if t > 0:
                        u = t - 1
                        dve.wait_ge(S(stage, "rs"), u + 1)
                        bufs_free(u)
                        v.scalar_tensor_tensor(dst[:, u % 2, :], xv[:, u, :], nrs[:, u:u + 1], gb, ALU.mult,
                                               ALU.mult).then_inc(S(stage, "hn"), 1)

            def hn_free(u):
                if u >= 2:
                    dve.wait_ge(S("n1", "tr"), 2 * (u - 1))

            norm_tokens("n1", g1b, hn, hn_free)
            dve.wait_ge(S("n1", "hn"), NT)
            dve.sem_inc(s_phd, 1)

            def reduce_sq(stage, j, heads, hd):
                dve.wait_ge(S(stage, "sq"), j + 1)
                if j >= 4:
                    dve.wait_ge(S(stage, "qn"), j - 3)
                link(v.tensor_reduce(ss[:, j % 4, 0:heads], sq[:, j % 2, :].rearrange("p (h d) -> p h d", h=heads),
                                     AX.X, ALU.add))
                mean_eps(ss[:, j % 4, 0:heads], ss[:, j % 4, 0:heads], hd, S(stage, "ss"))

            def scale_q(stage, j, src, heads, hd):
                dve.wait_ge(S(stage, "rs"), j + 1)
                if j >= 2:
                    dve.wait_ge(S(stage, "tr"), j - 1)
                r = rs[:, j % 4, 0:heads].unsqueeze(2).to_broadcast((P, heads, hd))
                return v.tensor_tensor(qn[:, j % 2, :].rearrange("p (h d) -> p h d", h=heads),
                                       src.rearrange("p (h d) -> p h d", h=heads), r, ALU.mult
                                       ).then_inc(S(stage, "qn"), 1)

            def project(stage):
                for j in range(18):
                    if j < 12:
                        reduce_sq(stage, j, 8, 64)
                    if 1 <= j <= 12:
                        scale_q(stage, j - 1, PS[:, (j - 1) % 4, :], 8, 64)
                        dve.wait_ge(S(stage, "qn"), j)
                        dve.sem_inc(S(stage, "pused"), 1)
                    if j >= 12:
                        dve.wait_ge(S(stage, "p"), j + 1)
                        v.tensor_copy(vv[:, j - 12, :], PS[:, j % 4, :]).then_inc(S(stage, "pused"), 1)
                dve.wait_ge(S(stage, "pused"), 18)
                dve.sem_inc(s_phd, 1)

            def attend(br):
                L = ATT[br]
                nm = 2 if br == "diff" else 1
                for step in range(len(L) + 3):
                    if step < len(L):
                        h, qt, t0, nt = L[step]
                        n = nt * P
                        nh = h if br == "diff" else 4 + h
                        b = nh % 2
                        if step % HPI == 0:
                            if br == "diff":
                                dve.wait_ge(s_b[b], 16 * (h // 2 + 1))
                            else:
                                dve.wait_ge(s_bm, h + 1)
                        dve.wait_ge(S(br, "log"), step + 1)
                        if step >= 3:
                            dve.wait_ge(S(br, "tr"), step - 2)
                        c0 = 384 - 128 * qt
                        for m in range(nm):
                            i = v.tensor_tensor(sT[:, step % 3, m, 0:n], PS[:, 2 * (step % 2) + m, 0:n],
                                                bias[:, b, c0:c0 + n], ALU.add)
                        i.then_inc(S(br, "biased"), 1)
                        dve.wait_ge(S(br, "biased"), step + 1)
                        v.tensor_reduce(mx[:, step % 3, 0:nm], sT[:, step % 3, 0:nm, 0:n], AX.X, ALU.max,
                                        negate=True).then_inc(S(br, "max"), 1)
                    a = step - 1
                    if 0 <= a < len(L):
                        n = L[a][3] * P
                        dve.wait_ge(S(br, "exp"), a + 1)
                        if br == "diff":
                            link(v.reciprocal(ri[:, a % 4, :], sm[:, a % 3, :]))
                            link(v.tensor_tensor(ri[:, a % 4, 1:2], ri[:, a % 4, 1:2], lam[:, 0:1], ALU.mult))
                            p2 = sT[:, a % 3, 1, 0:n]
                            link(v.tensor_scalar(p2, p2, ri[:, a % 4, 1:2], None, ALU.mult))
                            v.scalar_tensor_tensor(sT[:, a % 3, 0, 0:n], sT[:, a % 3, 0, 0:n], ri[:, a % 4, 0:1], p2,
                                                   ALU.mult, ALU.subtract).then_inc(S(br, "probs"), 1)
                        else:
                            v.reciprocal(ri[:, a % 4, 0:1], sm[:, a % 3, 0:1]).then_inc(S(br, "probs"), 1)
                    a = step - 3
                    if 0 <= a < len(L):
                        h, qt, t0, nt = L[a]
                        dve.wait_ge(S(br, "pv"), a + 1)
                        w = P if br == "diff" else 64
                        dst = y_tok[:, t0 + qt, h * w:(h + 1) * w]
                        if br == "diff":
                            i = v.tensor_copy(dst, PS[:, 6 + a % 2, 0:w])
                        else:
                            i = v.tensor_scalar(dst, PS[:, 6 + a % 2, 0:w], ri[:, a % 4, 0:1], None, ALU.mult)
                        i.then_inc(S(br, "out"), 1)
                dve.wait_ge(S(br, "out"), len(L))
                dve.sem_inc(s_phd, 1)

            project("pd")
            attend("diff")
            for j in range(NT + 1):
                if j < NT:
                    reduce_sq("yd", j, 4, 128)
                if j > 0:
                    scale_q("yd", j - 1, y_tok[:, j - 1, :], 4, 128)
            dve.wait_ge(S("yd", "qn"), NT)
            dve.sem_inc(s_phd, 1)
            project("pn")
            attend("na")
            dve.sem_inc(s_phd, 1)
            for s in range(16):
                j, hf = divmod(s, 2)
                cols = slice(hf * 384, hf * 384 + 384)
                dve.wait_ge(S("g", "sig"), 2 * s + 1)
                dve.wait_ge(S("g", "prod"), 4 * s + 3)
                v.tensor_tensor(mT[:, j, cols], gtmp[:, 2 * (s % 2), :], PS[:, 4 * (s % 2) + 2, 0:384], ALU.mult)
                dve.wait_ge(S("g", "sig"), 2 * s + 2)
                dve.wait_ge(S("g", "prod"), 4 * s + 4)
                g1 = gtmp[:, 2 * (s % 2) + 1, :]
                link(v.tensor_tensor(g1, g1, PS[:, 4 * (s % 2) + 3, 0:384], ALU.mult))
                v.tensor_tensor(mT[:, j, cols], mT[:, j, cols], g1, ALU.add).then_inc(S("g", "merged"), 1)
            dve.wait_ge(S("g", "merged"), 16)
            dve.sem_inc(s_phd, 1)
            for j in range(2 * NT):
                c, t = divmod(j, NT)
                dve.wait_ge(S("o", "prod"), j + 1)
                xs = xv[:, t, c * 512:(c + 1) * 512]
                v.tensor_tensor(xs, xs, PS[:, j % 8, :], ALU.add).then_inc(S("o", "added"), 1)
            dve.wait_ge(S("o", "added"), 12)
            dve.sem_inc(s_phd, 1)
            dve.wait_ge(S("rt", "g2"), 16)

            def tn_free(u):
                if u >= 2:
                    dve.wait_ge(S("n2", "tr"), 2 * (u - 1))
                    dve.wait_ge(S("n2", f"stored{u % 2}"), 16 * (u // 2))

            norm_tokens("n2", g2b, tn, tn_free)
            dve.wait_ge(S("rt", "logits"), NT)
            lg = PS[:, 4, 0:NT * E].rearrange("p (t e) -> p t e", t=NT)
            v.tensor_copy(aff, lg)
            v.tensor_reduce(rmx, lg, AX.X, ALU.max, negate=True).then_inc(S("rt", "shift"), 1)
            dve.wait_ge(S("rt", "exp"), 1)
            link(v.reciprocal(rrs, rsm))
            v.tensor_tensor(aff, aff, rrs.unsqueeze(2).to_broadcast((P, NT, E)), ALU.mult).then_inc(S("rt", "aff"), 1)
            dve.wait_ge(S("rt", "aff"), 1)
            v.tensor_copy(R[:, :, :, 1], aff)
            v.tensor_copy(R[:, :, :, 0], tokid.unsqueeze(2).to_broadcast((P, NT, E)))
            v.memset(ones, 1.0)
            dve.wait_ge(S("rt", "affT"), 1)
            link(v.tensor_copy(affT[:, 0:512], PS[0:E, 5, :]))
            link(v.tensor_copy(affT[:, 512:768], PS[0:E, 6, 0:256]))
            link(v.tensor_copy(work, affT))
            for lo, hi, cap in ((0, SP_, CP), (SP_, N, CS)):
                for r in range(cap // 8):
                    link(v.max(m8, work[:, lo:hi]))
                    link(v.match_replace(work[:, lo:hi], m8, work[:, lo:hi], -1.0))
            link(v.tensor_tensor(selT, affT, work, ALU.not_equal))
            for lo, hi in ((0, SP_), (SP_, N)):
                link(v.tensor_tensor_scan(cumT[:, lo:hi], ones[:, 0:hi - lo], selT[:, lo:hi], 0.0, ALU.mult, ALU.add))
            v.tensor_tensor(cumT, cumT, selT, ALU.mult).then_inc(S("rt", "rank"), 1)
            dve.wait_ge(S("rt", "rkT"), 1)
            link(v.tensor_copy(rk, PS[:, 7, 0:NT * E].rearrange("p (t e) -> p t e", t=NT)))
            for t in range(NT):
                w = CS if t >= 2 else CP
                if t >= 2:
                    dve.wait_ge(S("rt", "slots"), t - 1)
                v.tensor_tensor(G[:, t % 2, :, 0:w], rk[:, t, :].unsqueeze(2).to_broadcast((P, E, w)),
                                slot1[:, 0:w].unsqueeze(1).to_broadcast((P, E, w)), ALU.is_equal
                                ).then_inc(S("rt", "G"), 1)
            v.memset(idxf[:, 16:17], 0.0)
            link(v.memset(gate_s[:, 16:17], 0.0))
            dve.wait_ge(S("rt", "slots"), NT)
            for p0, w, b in ((0, CS, 1), (CS, CP, 0)):
                tab = PS[p0:p0 + w, b, 0:2 * E].rearrange("p (e c) -> p e c", c=2)
                v.tensor_copy(idxf[p0:p0 + w, 0:E], tab[:, :, 0])
                i = v.tensor_copy(gate_s[p0:p0 + w, 0:E], tab[:, :, 1])
            link(i)
            link(v.tensor_copy(idxi[:, :], idxf[:, :]))
            v.tensor_copy(cur_i[:, :], idxi[:, 0:1]).then_inc(S("x", "cur"), 1)
            dve.wait_ge(S("x", "cur"), 1)
            dve.sem_inc(S("rt", "tables_done"), 1)
            dve.sem_inc(s_phd, 1)

            TILES = [(0, 4), (4, 4), (8, FT - 8)]
            def xeT_evac(n):
                dve.wait_ge(S("x", "xe_t"), n)
                v.tensor_copy(xeT[:, 4:8, :], PS[:, 6, 0:4 * CAP].rearrange("p (k s) -> p k s", k=4)
                              ).then_inc(S("x", "xeT"), 1)

            dve.wait_ge(S("x", "iota"), 1)
            xeT_evac(2)
            with dve.Fori(0, E) as e:
                dve.wait_ge(S("x", "scattered"), e * 12 + 1)
                v.tensor_copy(cur_f[:, :], idxf[:, bass.ds(e, 1)])
                v.tensor_copy(cur_g[:, :], gate_s[:, bass.ds(e, 1)])
                dve.wait_ge(S("x", "xe"), e * 16 + 16)
                v.tensor_copy(cur_i[:, :], idxi[:, bass.ds(e + 1, 1)]).then_inc(S("x", "cur"), 1)
                dve.wait_ge(S("x", "cur"), e + 2)
                v.tensor_scalar(scat, iota_tok, cur_f[:, 0:1], None, ALU.is_equal).then_inc(S("x", "onehot"), 1)
                for h in range(2):
                    for g, (f0, nf) in enumerate(TILES):
                        dve.wait_ge(S("x", "up_group"), e * 6 + 3 * h + g + 1 + 1)
                        v.tensor_tensor(hT2[:, f0:f0 + nf, :], hg[:, f0:f0 + nf, :],
                                        PS[:, g, 0:nf * CAP].rearrange("p (f s) -> p f s", f=nf), ALU.mult
                                        ).then_inc(S("x", "hidden"), 1)
                xeT_evac(e * 2 + 4)
                dve.wait_ge(S("x", "down_bank"), e * 4 + 4 + 1)
                v.tensor_copy(yT[:, 4:8, :], PS[:, 4, 0:4 * CAP].rearrange("p (k s) -> p k s", k=4)
                              ).then_inc(S("x", "yT1"), 1)
                dve.wait_ge(S("x", "y_t"), e * 2 + 2)
                v.tensor_scalar(ye[:, 512:1024], PS[0:CAP, 6, :], cur_g[:, 0:1], None, ALU.mult
                                ).then_inc(S("x", "ye"), 1)
                for j in range(12):
                    t, half = divmod(j, 2)
                    dve.wait_ge(S("x", "scattered"), e * 12 + j + 1 + 1)
                    xs = xv[:, t, half * 512:(half + 1) * 512]
                    v.tensor_tensor(xs, xs, PS[:, 5 + j % 3, :], ALU.add).then_inc(S("x", "added"), 1)


_INS = ["x_prompt", "x_sample", "norm1_g", "w_in", "diff_q_norm", "diff_k_norm", "lambda_q1", "lambda_k1",
        "lambda_q2", "lambda_k2", "diff_subln_g", "rel_bias", "na_q_norm", "na_k_norm", "na_rpb", "w_branch_diff",
        "w_branch_na", "w_out", "norm2_g", "w_router", "w_expert_gate", "w_expert_up", "w_expert_down"]
_KEEP2D = {"norm1_g", "norm2_g", "diff_q_norm", "diff_k_norm", "lambda_q1", "lambda_k1", "lambda_q2", "lambda_k2",
           "diff_subln_g", "rel_bias", "na_q_norm", "na_k_norm"}


def _constants():
    import numpy as np
    c = np.zeros((P, C_W), np.float32)
    c[:, C_ID:C_ID + 128] = np.eye(P)
    col = np.arange(P) % 64
    start = np.clip(col - 8, 0, 48)[:, None]
    kc = np.arange(64)[None, :]
    c[:, C_MASK:C_MASK + 64] = np.where((kc >= start) & (kc < start + 16), 0.0, -1e30)
    c[:, C_TOK:C_TOK + NT] = np.arange(NT)[None, :] * P + np.arange(P)[:, None]
    c[:, C_SLOT:C_SLOT + 64] = 1 + np.arange(64)
    c[:, C_POW:C_POW + 64] = -0.5
    rel = np.arange(1024) - 511
    n = np.abs(rel)
    f = np.float32
    large = 8 + (np.log(np.maximum(n, 1).astype(f) / f(8)) / f(math.log(16.0)) * f(8)).astype(np.int32)
    bucket = np.where(rel > 0, 16, 0) + np.where(n < 8, n, np.minimum(large, 15))
    onehot = (np.arange(32)[:, None] == bucket[None, :]).astype(f)
    return c, onehot


def kernel(**inputs):
    import numpy as np
    import concourse.bacc as bacc
    from concourse.bass_utils import run_bass_kernel_spmd

    nc = bacc.Bacc("TRN2", target_bir_lowering=False, num_devices=1)
    arrays, args = {}, []

    def give(name, a):
        arrays[name] = a
        args.append(nc.dram_tensor(name, a.shape, mybir.dt.from_np(a.dtype), kind="ExternalInput").ap())

    for name in _INS:
        a = np.ascontiguousarray(inputs[name])
        give(f"in_{name}", a if name in _KEEP2D else a.reshape(a.shape[1:]))
    cst, onehot = _constants()
    give("in_consts", cst)
    give("in_t5_onehot", onehot)
    args.append(nc.dram_tensor("out_prompt", (SP_, D), F32, kind="ExternalOutput").ap())
    args.append(nc.dram_tensor("out_sample", (SS, D), F32, kind="ExternalOutput").ap())
    encoder(nc, *args)
    r = run_bass_kernel_spmd(nc, [arrays], core_ids=[0])
    out = r.results[0]
    return out["out_prompt"].reshape(1, SP_, D), out["out_sample"].reshape(1, SS, D)
```

```python
import math
from contextlib import ExitStack

import concourse.bass as bass
from concourse import mybir

P = 128
D = 1024
SP_, SS = 256, 512
N = SP_ + SS
NT = N // P
KD = D // P
HW = 512
FF = 2816
E = 16
HF = FF // 2
QF = FF // 4
QC = QF // 2
FT = HF // P
CP, CS = 2 * SP_ // E, 2 * SS // E
CAP = CP + CS
EPS = 1e-6
LAM0 = 0.8 - 0.6 * math.exp(0.0)
BW = 896
NA_ROWS = 15
GROUPS = [(0, 2), (2, 4)]

F32 = mybir.dt.float32
F32R = mybir.dt.float32r
I32 = mybir.dt.int32
ALU = mybir.AluOpType
ACT = mybir.ActivationFunctionType
AX = mybir.AxisListType

C_ID, C_MASK, C_TOK, C_SLOT, C_POW = 0, 128, 192, 198, 262
C_W = C_POW + 64

UNIT = 4 * 512
CHUNKS = []
for _stage, _kinds in (("pd", ("q", "k", "v")), ("pn", ("q", "k", "v")),
                       ("g", ("gate_d0", "br_d0", "gate_d1", "br_d1", "gate_n0", "br_n0", "gate_n1", "br_n1")),
                       ("o", ("out0", "out1"))):
    for _kind in _kinds:
        _at = CHUNKS[-1][2] + CHUNKS[-1][3] if CHUNKS else 0
        CHUNKS.append((_stage, _kind, _at, 1 if _kind[:2] == "br" else 2))
UNITS = CHUNKS[-1][2] + CHUNKS[-1][3]

XU = []
for _q in range(4):
    XU += [("gate", _q, 0), ("gate", _q, 1)]
    if _q == 2:
        XU += [("down", 0, _c) for _c in range(4)]
    XU += [("up", _q, 0), ("up", _q, 1)]
XU += [("down", 1, _c) for _c in range(4)]
NXU = len(XU)
XUNIT = 3 * D
DT = [(0, 2), (2, 3), (5, 3), (8, 3)]
HR = [(0, 5), (5, 3), (8, 3)]
RAWS, SPLITS = 4, 3


def after(kind, part, c=1):
    return XU.index((kind, part, c))


MISC = {after("gate", 1): [("hidden", 0)], after("gate", 2, 0): [("hidden", 1)], after("gate", 2): [("hidden", 2)],
        after("gate", 3, 0): [("hidden", 3)], after("up", 3): [("tokens", 0)],
        after("down", 1, 0): [("hidden", 4)], after("down", 1, 1): [("hidden", 5), ("tokens", 1)]}
for _j, _w in enumerate([_w for _w in range(2, NXU) if _w not in MISC][:12]):
    MISC[_w] = [("scatter", _j)]
USES = [(w, m) for w in sorted(MISC) for m in MISC[w]]
NU = len(USES)
PRE = 2
NH_ = sum(m[0] != "scatter" for _, m in USES)


def use_no(kind, i):
    return [m for _, m in USES].index((kind, i))


def encoder(nc, x_prompt, x_sample, norm1_g, w_in, diff_q_norm, diff_k_norm, lambda_q1, lambda_k1, lambda_q2,
            lambda_k2, diff_subln_g, rel_bias, na_q_norm, na_k_norm, na_rpb, w_branch_diff, w_branch_na, w_out,
            norm2_g, w_router, w_expert_gate, w_expert_up, w_expert_down, consts, t5_onehot, y_prompt, y_sample):
    ctx = ExitStack()
    with ctx:
        BASE = -(-nc.sbuf_base // 64) * 64

        def at(name, off, cols, parts=P, dt=F32):
            return nc.alloc_sbuf_tensor_at(name, [parts, cols], dt, offset=BASE + 4 * off)[:, :]

        def sem(name):
            return ctx.enter_context(nc.semaphore(name))

        cst = at("cst", 0, C_W)
        small = at("small", 328, 400)
        wrt_v = at("wrt", 728, KD * E).rearrange("p (k e) -> p k e", k=KD)
        idxf = at("idxf", 856, E + 1, CAP)
        gate_s = at("gate_s", 880, E + 1, CAP)
        idxi = at("idxi", 904, E + 1, CAP, I32)
        cur_f = at("cur_f", 928, 1, CAP)
        cur_g = at("cur_g", 936, 1, CAP)
        xv = at("x", 960, NT * D).rearrange("p (t d) -> p t d", t=NT)
        y_tok = {"diff": at("yd", 960, NT * HW).rearrange("p (t n) -> p t n", t=NT),
                 "na": at("yn", 960 + 3072, NT * HW).rearrange("p (t n) -> p t n", t=NT)}
        hTh = at("hT_high", 7104, 6144, dt=F32R).rearrange("p (k n) -> p k n", k=KD)
        hTl = at("hT_low", 13248, 6144, dt=F32R).rearrange("p (k n) -> p k n", k=KD)
        wraw = at("w_raw", 19392, 2 * UNIT).rearrange("p (b k n) -> p b k n", b=2, k=4)
        wh = at("w_high", 23488, 2 * UNIT, dt=F32R).rearrange("p (b k n) -> p b k n", b=2, k=4)
        wl = at("w_low", 27584, 2 * UNIT, dt=F32R).rearrange("p (b k n) -> p b k n", b=2, k=4)
        qT = at("qT", 31680, 3072).rearrange("p (c n) -> p c n", c=4)
        kT = at("kT", 34752, 3072).rearrange("p (c n) -> p c n", c=4)
        vv = at("v", 37824, 3072).rearrange("p (t n) -> p t n", t=NT)
        sT = at("s", 40896, 4096).rearrange("p (b m n) -> p b m n", b=4, m=2)
        sq = at("sq", 40896, 1024).rearrange("p (b n) -> p b n", b=2)
        qn = at("qn", 41920, 1024).rearrange("p (b n) -> p b n", b=2)
        bias = at("bias", 44992, 2 * BW).rearrange("p (b n) -> p b n", b=2)
        aT = at("aT", 46784, 1024).rearrange("p (b n) -> p b n", b=2)
        hn = at("hn", 31680, 2048).rearrange("p (b n) -> p b n", b=2)
        junk = at("junk", 33728, 1024)
        g1b = at("g1b", 37824, 1024)
        napad = at("napad", 47808, 128, 120)
        t5h = at("t5h", 47936, 1024, 32)
        t5b = at("t5b", 48960, 1024, 4)
        t5t = at("t5t", 49984, 4, 32)
        lamv = at("lamv", 50048, 256).rearrange("p (v d) -> p v d", v=4)
        yTh = at("yT_high", 31680, 3072, dt=F32R).rearrange("p (c n) -> p c n", c=4)
        yTl = at("yT_low", 34752, 3072, dt=F32R).rearrange("p (c n) -> p c n", c=4)
        mm_ = at("merged", 37824, NT * D).rearrange("p (t n) -> p t n", t=NT)
        sg_n = at("sig_na", 43968, NT * HW).rearrange("p (t n) -> p t n", t=NT)
        tn = at("tn", 7104, 2048).rearrange("p (b n) -> p b n", b=2)
        tT = at("tT", 9152, 2048).rearrange("p (b k n) -> p b k n", b=2, k=KD)
        g2b = at("g2b", 11200, 1024)
        G = at("G", 12224, 2048).rearrange("p (b e s) -> p b e s", b=2, e=E)
        rk = at("rk", 14272, 96).rearrange("p (t e) -> p t e", t=NT)
        R = at("R", 14368, 192).rearrange("p (t e c) -> p t e c", t=NT, c=2)
        junk2 = at("junk2", 19392, 1024)
        affT = at("affT", 48704, 768, E)
        work = at("work", 49472, 768, E)
        selT = at("selT", 50240, 768, E)
        cumT = at("cumT", 51008, 768, E)
        ones = at("ones", 51776, 512, E)
        xl = at("x_w_low", 7104, SPLITS * XUNIT, dt=F32R).rearrange("p (b n) -> p b n", b=SPLITS)
        xh = at("x_w_high", 16320, SPLITS * XUNIT, dt=F32R).rearrange("p (b n) -> p b n", b=SPLITS)
        xTh = at("xT_high", 25536, KD * CAP, dt=F32R)
        xTl = at("xT_low", 26304, KD * CAP, dt=F32R)
        hidh = at("hidden_high", 27072, FT * CAP, dt=F32R)
        hidl = at("hidden_low", 28128, FT * CAP, dt=F32R)
        yeh = at("y_high", 29184, D, CAP, dt=F32R)
        yel = at("y_low", 30208, D, CAP, dt=F32R)
        xraw = at("x_w_raw", 31680, RAWS * XUNIT).rearrange("p (b n) -> p b n", b=RAWS)
        scat = at("scatter_onehot", 43968, N, CAP, dt=F32R)
        xe = at("gathered", 44736, D, CAP)
        hid = at("hidden", 45760, HF, CAP)
        sg = at("silu", 47168, QF, CAP)
        iota_tok = at("iota_tok", 47872, N, CAP)

        ident = cst[:, C_ID:C_ID + 128]
        mask = cst[:, C_MASK:C_MASK + 64]
        tokid = cst[:, C_TOK:C_TOK + NT]
        slot1 = cst[:, C_SLOT:C_SLOT + 64]
        mhalf = cst[:, C_POW:C_POW + 64]

        ss = small[:, 0:32].rearrange("p (b n) -> p b n", b=4)
        rs = small[:, 32:64].rearrange("p (b n) -> p b n", b=4)
        nss = small[:, 64:70]
        nrs = small[:, 72:78]
        mx = small[:, 80:88].rearrange("p (b m) -> p b m", b=4)
        sm = small[:, 88:96].rearrange("p (b m) -> p b m", b=4)
        ri = small[:, 96:112].rearrange("p (b m) -> p b m", b=8)
        lam = small[:, 112:116]
        gains = small[:, 120:128]
        rmx = small[:, 128:134]
        rsm = small[:, 136:142]
        rrs = small[:, 144:150]
        m8 = small[0:E, 152:160]
        aff = small[:, 200:296].rearrange("p (t e) -> p t e", t=NT)

        PS = ctx.enter_context(nc.psum_tensor("PS", [P, 8, 512], F32))
        t5_dram = nc.dram_tensor("t5_dram", [4, 1024], F32, kind="Internal").ap()
        na_dram = nc.dram_tensor("na_dram", [120, 128], F32, kind="Internal").ap()
        t5_rep = nc.dram_tensor("t5_rep", [4, P, 1024], F32, kind="Internal").ap()
        na_rep = nc.dram_tensor("na_rep", [8, 64, NA_ROWS * 128], F32, kind="Internal").ap()
        t_dram = nc.dram_tensor("t_dram", [N, D], F32, kind="Internal").ap()

        s_x = [sem(f"x_loaded{t}") for t in range(NT)]
        s_cst = sem("constants_loaded")
        s_lamv = sem("lambdas_loaded")
        s_tab = sem("tables_loaded")
        s_nz = sem("na_pad_zeroed")
        s_nt = sem("na_table_in_pad")
        s_tm = sem("t5_rows_ready")
        s_tc = sem("t5_rows_in_sbuf")
        s_scr = sem("bias_rows_in_dram")
        s_rep = sem("bias_rows_replicated")
        s_b = [sem(f"bias_loaded{b}") for b in range(2)]
        s_bm = sem("bias_masked")
        s_pha = sem("act_done_with_stage")
        s_phd = sem("dve_done_with_stage")
        s_dv = sem("dve_chain")
        s_lam = sem("lambda_sums_ready")
        s_lae = sem("lambda_exps_ready")
        w_loaded = [sem(f"unit_loaded{b}") for b in range(2)]
        w_high = sem("unit_high_ready")
        w_split = sem("unit_split_ready")
        w_prod = sem("unit_tile_products")
        x_loaded = [sem(f"x_unit_loaded{b}") for b in range(RAWS)]
        x_high = sem("x_unit_high_ready")
        x_split = sem("x_unit_split_ready")
        x_used = sem("x_unit_used")

        sems = {}

        def S(stage, name):
            k = f"{stage}_{name}"
            if k not in sems:
                sems[k] = sem(k)
            return sems[k]

        chain_count = [0]

        def xsrc(a, b, t):
            return a[t * P:(t + 1) * P, :] if t < 2 else b[(t - 2) * P:(t - 1) * P, :]

        def items(heads):
            return [(h, qt, t0, nt) for h in range(heads) for (t0, nt) in GROUPS for qt in range(nt)]

        ATT = {"diff": items(4), "na": items(8)}
        HPI = NT

        def stage_done(eng, k):
            eng.wait_ge(s_pha, k)
            eng.wait_ge(s_phd, k)

        def product_done(eng, chunk, t):
            eng.wait_ge(w_prod, NT * (chunk[2] + chunk[3] - 1) + t + 1)

        def unit_width(w):
            return DT[XU[w][2]][1] * D if XU[w][0] == "down" else 4 * QF

        block = ctx.enter_context(nc.Block())

        @block.sync
        def _(sp):
            for t in range(NT):
                sp.dma_start(xv[:, t, :], xsrc(x_prompt, x_sample, t)).then_inc(s_x[t], 16)

            def src_of(stage, kind, u):
                if kind[:2] == "br":
                    src, c0 = {"d": w_branch_diff, "n": w_branch_na}[kind[3]], 512 * int(kind[4])
                elif stage == "o":
                    src, c0 = w_out, 512 * int(kind[3])
                elif stage == "g":
                    src, c0 = w_in, 6 * HW + {"d": 0, "n": D}[kind[5]] + 512 * int(kind[6])
                else:
                    src, c0 = w_in, HW * ({"pd": 0, "pn": 3}[stage] + "qkv".index(kind))
                return src[u * 512:(u + 1) * 512, c0:c0 + 512].rearrange("(k p) c -> p k c", p=P)

            for stage, kind, u0, nu in CHUNKS:
                for u in range(u0, u0 + nu):
                    if u >= 2:
                        sp.wait_ge(w_split, u - 1)
                    sp.dma_start(wraw[:, u % 2], src_of(stage, kind, u - u0)).then_inc(w_loaded[u % 2], 16)
                if kind == "out0":
                    sp.wait_ge(S("g", "yn_t"), NT)
                    for t in range(NT):
                        sp.dma_start(xv[:, t, :], xsrc(x_prompt, x_sample, t)).then_inc(s_x[t], 16)
            gate_src = w_expert_gate.rearrange("e (k p) f -> e p k f", p=P)
            up_src = w_expert_up.rearrange("e (k p) f -> e p k f", p=P)
            down_src = w_expert_down.rearrange("e (f p) d -> e p f d", p=P)
            stage_done(sp, 6)
            sp.wait_ge(S("o", "m_t"), 2 * NT)
            with sp.Fori(0, E) as e:
                for w, (kind, q, c) in enumerate(XU):
                    sp.wait_ge(x_split, e * NXU + w + 1)
                    b = w % RAWS
                    if kind == "down":
                        f0, nf = DT[c]
                        src = down_src[e, :, q * FT + f0:q * FT + f0 + nf, :]
                        dst = xraw[:, b, 0:nf * D].rearrange("p (f d) -> p f d", f=nf)
                    else:
                        src = (gate_src if kind == "gate" else up_src)[e, :, 4 * c:4 * c + 4, q * QF:(q + 1) * QF]
                        dst = xraw[:, b, 0:4 * QF].rearrange("p (k f) -> p k f", k=4)
                    sp.dma_start(dst, src).then_inc(x_loaded[b], 16)
            for t in range(NT):
                sp.wait_ge(S("x", "last_added"), 2 * t + 2)
                sp.dma_start(xsrc(y_prompt, y_sample, t), xv[:, t, :]).then_inc(S("x", "stored"), 16)
            sp.wait_ge(S("x", "stored"), 16 * NT)

        @block.gpsimd
        def _(pool):
            pool.dma_start(cst, consts).then_inc(s_cst, 16)
            pool.dma_start(g1b, norm1_g.to_broadcast((P, D))).then_inc(s_cst, 16)
            nc.gpsimd.memset(napad, 0.0).then_inc(s_nz, 1)
            for i, v in enumerate((lambda_q1, lambda_k1, lambda_q2, lambda_k2)):
                pool.dma_start(lamv[:, i, :], v.to_broadcast((P, 64))).then_inc(s_lamv, 16)
            for col, g, w in ((0, diff_q_norm, 64), (1, diff_k_norm, 64), (2, diff_subln_g, 128), (3, na_q_norm, 64),
                              (4, na_k_norm, 64)):
                for r in range(P // w):
                    pool.dma_start(gains[r * w:(r + 1) * w, col:col + 1],
                                   g.rearrange("a d -> d a")).then_inc(s_lamv, 16)
            pool.dma_start(t5h, t5_onehot).then_inc(s_tab, 16)
            pool.dma_start(t5t, rel_bias).then_inc(s_tab, 16)
            pool.wait_ge(s_nz, 1)
            pool.dma_start(napad[:, 48:79], na_rpb.rearrange("h r c -> (h r) c")).then_inc(s_nt, 16)
            pool.wait_ge(s_cst, 32)

            def rsqrt(out, in_, w, wait, val, done):
                pool.wait_ge(wait, val)
                nc.gpsimd.tensor_tensor(out, in_, mhalf[:, 0:w], ALU.pow).then_inc(done, 1)

            for t in range(NT):
                rsqrt(nrs[:, t:t + 1], nss[:, t:t + 1], 1, S("n1", "ss"), t + 1, S("n1", "rs"))
            pool.wait_ge(s_nt, 16)
            pool.dma_start(na_dram, napad).then_inc(s_scr, 16)
            pool.wait_ge(s_tc, 1)
            pool.dma_start(t5_dram, t5b).then_inc(s_scr, 16)
            pool.wait_ge(s_scr, 32)
            t5_src = bass.AP(t5_dram.tensor, 0, [[1024, 4], [0, P], [1, 1024]])
            na_src = bass.AP(na_dram.tensor, 0, [[NA_ROWS * 128, 8], [0, 64], [1, NA_ROWS * 128]])
            pool.dma_start(t5_rep, t5_src).then_inc(s_rep, 16)
            pool.dma_start(na_rep, na_src).then_inc(s_rep, 16)
            pool.dma_start(wrt_v, w_router.rearrange("(k p) e -> p k e", p=P)).then_inc(S("rt", "wrt"), 16)

            def load_bias(nh):
                b = nh % 2
                if nh == 0:
                    pool.wait_ge(s_rep, 32)
                if nh >= 2:
                    br, used = ("diff", nh - 1) if nh - 2 < 4 else ("na", nh - 5)
                    pool.wait_ge(S(br, "biased"), HPI * used)
                if nh < 4:
                    src = bass.AP(t5_rep.tensor, nh * P * 1024 + 127, [[1023, 128], [1, BW]])
                    pool.dma_start(bias[:, b, :], src).then_inc(s_b[b], 16)
                else:
                    h = nh - 4
                    for rr in range(2):
                        src = bass.AP(na_rep.tensor, (h * 64 * NA_ROWS + 1 - rr) * 128 + 63,
                                      [[NA_ROWS * 128 - 1, 64], [128, 14], [1, 64]])
                        pool.dma_start(bias[64 * rr:64 * rr + 64, b, :].rearrange("p (j k) -> p j k", j=14),
                                       src).then_inc(s_b[b], 16)

            def mask_bias(nh):
                b = nh % 2
                pool.wait_ge(s_b[b], 32 * (nh // 2 - 2) + 64)
                v = bias[:, b, :].rearrange("p (j k) -> p j k", j=14)
                nc.gpsimd.tensor_tensor(v, v, mask.unsqueeze(1).to_broadcast((P, 14, 64)), ALU.add).then_inc(s_bm, 1)

            def norm_rs(stage, jobs, w):
                for j in range(jobs):
                    rsqrt(rs[:, j % 4, 0:w], ss[:, j % 4, 0:w], w, S(stage, "ss"), j + 1, S(stage, "rs"))

            load_bias(0)
            load_bias(1)
            norm_rs("pd", 12, 8)
            load_bias(2)
            load_bias(3)
            load_bias(4)
            load_bias(5)
            norm_rs("yd", NT, 4)
            mask_bias(4)
            mask_bias(5)
            norm_rs("pn", 12, 8)
            for nh in range(6, 12):
                load_bias(nh)
                mask_bias(nh)
            stage_done(pool, 7)
            pool.dma_start(g2b, norm2_g.to_broadcast((P, D))).then_inc(S("rt", "g2"), 16)
            for t in range(NT):
                rsqrt(nrs[:, t:t + 1], nss[:, t:t + 1], 1, S("n2", "ss"), t + 1, S("n2", "rs"))
                pool.wait_ge(S("n2", "hn"), t + 1)
                pool.dma_start(t_dram[t * P:(t + 1) * P, :], tn[:, t % 2, :]).then_inc(S("n2", f"stored{t % 2}"), 16)
            nc.gpsimd.iota(iota_tok, pattern=[[1, N]], base=0, channel_multiplier=0,
                           allow_small_or_imprecise_dtypes=True).then_inc(S("x", "iota"), 1)
            pool.wait_ge(S("n2", "stored0"), 48)
            pool.wait_ge(S("n2", "stored1"), 48)
            pool.wait_ge(S("rt", "tables"), 1)
            for e in range(E + 1):
                if e == 1:
                    pool.wait_ge(S("x", "misc"), PRE)
                elif e > 1:
                    pool.wait_ge(S("x", "misc"), PRE + NU * (e - 2) + use_no("tokens", 1) + 1)
                col = min(e, E - 1) + 1
                pool.indirect_dma_start(xe, None, t_dram, bass.IndirectOffsetOnAxis(ap=idxi[:, col:col + 1], axis=0)
                                        ).then_inc(S("x", "xe"), 16)
            pool.wait_ge(S("x", "xe"), 16 * (E + 1))

        @block.tensor
        def _(pe):
            mm = nc.tensor.matmul
            pe.sem_inc(x_used, SPLITS)
            pe.wait_ge(s_cst, 32)
            pe.wait_ge(s_tab, 32)
            for b in range(2):
                i = mm(PS[0:4, 6 + b, :], t5t, t5h[:, b * 512:(b + 1) * 512], start=True, stop=True)
            i.then_inc(s_tm, 1)

            def split_product(out, sh, sl, mh, ml, first, last):
                mm(out, sh, mh, start=first, stop=False)
                mm(out, sh, ml, start=False, stop=False)
                return mm(out, sl, mh, start=False, stop=last)

            for t in range(NT):
                pe.wait_ge(S("n1", "hn"), t + 1)
                for q in range(2):
                    j = 2 * t + q
                    if j >= 4:
                        pe.wait_ge(S("n1", "tev"), j - 3)
                    for k in range(4):
                        i = nc.tensor.transpose(PS[:, j % 4, k * P:(k + 1) * P],
                                                hn[:, t % 2, (4 * q + k) * P:(4 * q + k + 1) * P], ident)
                    i.then_inc(S("n1", "tr"), 1)

            def transposes(stage, jt, src, done):
                if jt >= 2:
                    pe.wait_ge(S(stage, "tev"), jt - 1)
                for c in range(4):
                    i = nc.tensor.transpose(PS[:, 6 + jt % 2, c * P:(c + 1) * P], src[:, c * P:(c + 1) * P], ident)
                i.then_inc(S(stage, done), 1)

            def chunk_steps(chunks):
                return [(c, u, t) for c in range(len(chunks)) for u in range(chunks[c][3]) for t in range(NT)]

            def chunk_product(chunks, c, u, t, sh, sl, bank_free):
                stage, kind, u0, nu = chunks[c]
                n = u0 + u
                if t == 0:
                    pe.wait_ge(w_split, n + 1)
                if u == 0:
                    bank_free(c, t)
                for k in range(4):
                    i = split_product(PS[:, t, :], sh[:, 4 * u + k, t * P:(t + 1) * P],
                                      sl[:, 4 * u + k, t * P:(t + 1) * P], wh[:, n % 2, k], wl[:, n % 2, k],
                                      u == 0 and k == 0, u == nu - 1 and k == 3)
                i.then_inc(w_prod, 1)

            def project(stage, k):
                stage_done(pe, k)
                chunks = [c for c in CHUNKS if c[0] == stage]
                steps = chunk_steps(chunks)

                def bank_free(c, t):
                    if c > 0:
                        pe.wait_ge(S(stage, "pused"), NT * (c - 1) + t + 1)

                done_at, jt = [], 0
                for n, (c, u, t) in enumerate(steps):
                    chunk_product(chunks, c, u, t, hTh, hTl, bank_free)
                    if u == 1 and c < 2:
                        done_at.append(n)
                    while jt < len(done_at) and n >= done_at[jt] + 2:
                        pe.wait_ge(S(stage, "qn"), jt + 1)
                        transposes(stage, jt, qn[:, jt % 2, :], "tr")
                        jt += 1

            def attend(br, k):
                stage_done(pe, k)
                L = ATT[br]
                nm = 2 if br == "diff" else 1
                for step in range(len(L) + 4):
                    if step < len(L):
                        h, qt, t0, nt = L[step]
                        if step >= 2:
                            pe.wait_ge(S(br, "biased"), step - 1)
                        for m in range(nm):
                            c, r = (h, m) if br == "diff" else (h // 2, h % 2)
                            i = mm(PS[:, 2 * (step % 2) + m, 0:nt * P],
                                   qT[64 * r:64 * r + 64, c, (t0 + qt) * P:(t0 + qt + 1) * P],
                                   kT[64 * r:64 * r + 64, c, t0 * P:(t0 + nt) * P], start=True, stop=True)
                        i.then_inc(S(br, "log"), 1)
                    a = step - 3
                    if 0 <= a < len(L):
                        h, qt, t0, nt = L[a]
                        pe.wait_ge(S(br, "probs"), a + 1)
                        if a >= 2:
                            pe.wait_ge(S(br, "aT"), a - 1)
                        for c in range(nt):
                            i = nc.tensor.transpose(PS[:, 4 + a % 2, c * P:(c + 1) * P],
                                                    sT[:, a % 4, 0, c * P:(c + 1) * P], ident)
                        i.then_inc(S(br, "tr"), 1)
                    a = step - 4
                    if 0 <= a < len(L):
                        h, qt, t0, nt = L[a]
                        pe.wait_ge(S(br, "aT"), a + 1)
                        if a >= 2:
                            pe.wait_ge(S(br, "out"), a - 1)
                        w = P if br == "diff" else 64
                        for c in range(nt):
                            i = mm(PS[:, 6 + a % 2, 0:w], aT[:, a % 2, c * P:(c + 1) * P],
                                   vv[:, t0 + c, h * w:(h + 1) * w], start=c == 0, stop=c == nt - 1)
                        i.then_inc(S(br, "pv"), 1)

            project("pd", 1)
            attend("diff", 2)
            project("pn", 3)
            attend("na", 4)
            stage_done(pe, 5)
            pe.wait_ge(S("yd", "qn"), NT)
            for t in range(NT):
                transposes("g", t, y_tok["diff"][:, t, :], "yd_t")
            chunks = [c for c in CHUNKS if c[0] == "g"]

            def g_bank_free(c, t):
                if c > 0:
                    kind = chunks[c - 1][1]
                    pe.wait_ge(S("g", "sig" if kind[:4] == "gate" else "mul"), NT * ((c - 1) // 2) + t + 1)

            for c, u, t in chunk_steps(chunks):
                kind = chunks[c][1]
                if kind == "gate_n0" and u == 0 and t == 0:
                    for v in range(NT):
                        j = NT + v
                        pe.wait_ge(S("g", "tev"), j - 1)
                        for q in range(4):
                            i = nc.tensor.transpose(PS[:, 6 + j % 2, q * P:(q + 1) * P],
                                                    y_tok["na"][:, v, q * P:(q + 1) * P], ident)
                        i.then_inc(S("g", "yn_t"), 1)
                if kind[:2] == "br" and u == 0 and t == 0:
                    pe.wait_ge(S("g", "tev"), NT if kind[3] == "d" else 2 * NT)
                sh, sl = (yTh, yTl) if kind[:2] == "br" else (hTh, hTl)
                chunk_product(chunks, c, u, t, sh, sl, g_bank_free)
            stage_done(pe, 6)
            for j in range(2 * NT):
                t, q = j % NT, j // NT
                if j >= 2:
                    pe.wait_ge(S("o", "tev"), j - 1)
                for k in range(4):
                    i = nc.tensor.transpose(PS[:, 6 + j % 2, k * P:(k + 1) * P],
                                            mm_[:, t, (4 * q + k) * P:(4 * q + k + 1) * P], ident)
                i.then_inc(S("o", "m_t"), 1)
            pe.wait_ge(S("o", "tev"), 2 * NT)
            chunks = [c for c in CHUNKS if c[0] == "o"]

            def o_bank_free(c, t):
                if c > 0:
                    pe.wait_ge(S("o", "added"), t + 1)

            for c, u, t in chunk_steps(chunks):
                chunk_product(chunks, c, u, t, hTh, hTl, o_bank_free)
            stage_done(pe, 7)
            pe.wait_ge(S("rt", "wrt"), 16)
            for t in range(NT):
                pe.wait_ge(S("n2", "hn"), t + 1)
                for q in range(2):
                    j = 2 * t + q
                    if j >= 4:
                        pe.wait_ge(S("n2", "tev"), j - 3)
                    for k in range(4):
                        i = nc.tensor.transpose(PS[:, j % 4, k * P:(k + 1) * P],
                                                tn[:, t % 2, (4 * q + k) * P:(4 * q + k + 1) * P], ident)
                    i.then_inc(S("n2", "tr"), 1)
                pe.wait_ge(S("n2", "tev"), 2 * t + 2)
                for k in range(KD):
                    i = mm(PS[:, 4, t * E:(t + 1) * E], tT[:, t % 2, k, :], wrt_v[:, k, :],
                           start=k == 0, stop=k == KD - 1)
                i.then_inc(S("rt", "logits"), 1)
            pe.wait_ge(S("rt", "aff"), 1)
            for t in range(NT):
                i = nc.tensor.transpose(PS[0:E, 5 + t // 4, (t % 4) * P:(t % 4 + 1) * P], aff[:, t, :], ident)
            i.then_inc(S("rt", "affT"), 1)
            pe.wait_ge(S("rt", "rank"), 1)
            for t in range(NT):
                i = nc.tensor.transpose(PS[:, 7, t * E:(t + 1) * E], cumT[:, t * P:(t + 1) * P], ident[0:E, 0:E])
            i.then_inc(S("rt", "rkT"), 1)
            for t in range(NT):
                pe.wait_ge(S("rt", "G"), t + 1)
                smp = t >= 2
                w, p0 = (CS, 0) if smp else (CP, CS)
                first = 2 if smp else 0
                last = NT - 1 if smp else 1
                for e in range(E):
                    i = mm(PS[p0:p0 + w, 1 if smp else 0, 2 * e:2 * e + 2], G[:, t % 2, e, 0:w], R[:, t, e, :],
                           start=(t == first and e == 0), stop=t == last, skip_group_check=True)
                i.then_inc(S("rt", "slots"), 1)

            def transpose_tokens(q):
                for k in range(4):
                    i = nc.tensor.transpose(PS[:, 6 + q % 2, k * CAP:(k + 1) * CAP],
                                            xe[:, (4 * q + k) * P:(4 * q + k + 1) * P], ident[0:CAP, 0:CAP])
                i.then_inc(S("x", "misc"), 1)

            def scatter(j, bank):
                t, half = divmod(j, 2)
                lhs = scat[:, t * P:(t + 1) * P]
                cols = slice(half * 512, (half + 1) * 512)
                mm(PS[:, bank, :], lhs, yeh[:, cols], start=True, stop=False)
                mm(PS[:, bank, :], lhs, yel[:, cols], start=False, stop=True).then_inc(S("x", "misc"), 1)

            stage_done(pe, 8)
            pe.wait_ge(S("x", "xe"), 16)
            for q in range(PRE):
                transpose_tokens(q)
            pe.wait_ge(S("x", "misc_read"), PRE)
            xT = [a.rearrange("p (k s) -> p k s", k=KD) for a in (xTh, xTl)]
            hT = [a.rearrange("p (f s) -> p f s", f=FT) for a in (hidh, hidl)]
            with pe.Fori(0, E) as e:
                for w, (kind, q, c) in enumerate(XU):
                    b = w % SPLITS
                    pe.wait_ge(x_split, e * NXU + w + 1 + RAWS)
                    if kind == "down":
                        f0, nf = DT[c]
                        uh, ul = (a[:, b, 0:nf * D].rearrange("p (f d) -> p f d", f=nf) for a in (xh, xl))
                        last_round = [r for r, (r0, rn) in enumerate(HR) if r0 < f0 + nf][-1]
                        pe.wait_ge(S("x", "misc_read"), e * NU + PRE + use_no("hidden", 3 * q + last_round) + 1)
                        for f in range(nf):
                            g = f0 + f
                            for half in range(2):
                                cols = slice(half * 512, (half + 1) * 512)
                                i = split_product(PS[0:CAP, 4 + half, :], hT[0][:, g, :], hT[1][:, g, :],
                                                  uh[:, f, cols], ul[:, f, cols], q == 0 and g == 0,
                                                  q == 1 and g == FT - 1)
                    else:
                        uh, ul = (a[:, b, 0:4 * QF].rearrange("p (k f) -> p k f", k=4) for a in (xh, xl))
                        if kind == "gate" and c == 0 and q > 0:
                            pe.wait_ge(S("x", "silu"), e * 4 + q)
                        b0 = 0 if kind == "gate" else 2
                        for k in range(4):
                            for half in range(2):
                                cols = slice(half * QC, (half + 1) * QC)
                                i = split_product(PS[0:CAP, b0 + half, 0:QC], xT[0][:, 4 * c + k, :],
                                                  xT[1][:, 4 * c + k, :], uh[:, k, cols], ul[:, k, cols],
                                                  c == 0 and k == 0, c == 1 and k == 3)
                    i.then_inc(x_used, 1)
                    for what, j in MISC.get(w, []):
                        u = use_no(what, j)
                        pe.wait_ge(S("x", "misc_read"), e * NU + PRE + u - 1)
                        if what == "tokens":
                            if j == 0:
                                pe.wait_ge(S("x", "xe"), e * 16 + 32)
                            transpose_tokens(j)
                        elif what == "hidden":
                            h, r = divmod(j, 3)
                            f0, nf = HR[r]
                            need = 2 * h + (1 if (f0 + nf) * P <= QF else 2)
                            pe.wait_ge(S("x", "hidden"), e * 4 + need)
                            for f in range(nf):
                                i = nc.tensor.transpose(PS[:, 6 + u % 2, f * CAP:(f + 1) * CAP],
                                                        hid[:, (f0 + f) * P:(f0 + f + 1) * P], ident[0:CAP, 0:CAP])
                            i.then_inc(S("x", "misc"), 1)
                        else:
                            if j == 0:
                                pe.wait_ge(S("x", "ye_low"), e + 1)
                                pe.wait_ge(S("x", "onehot"), e + 1)
                            scatter(j, 6 + u % 2)
            pe.wait_ge(S("x", "onehot"), E + 1)
            pe.wait_ge(S("x", "ye_low"), E + 1)
            for j in range(12):
                pe.wait_ge(S("x", "misc_read"), E * NU + PRE + j - 1)
                scatter(j, 6 + j % 2)

        @block.scalar
        def _(act):
            a_ = nc.scalar.activation
            unit = [0]

            def split_units(upto):
                while unit[0] < min(upto, UNITS):
                    n = unit[0]
                    act.wait_ge(w_loaded[n % 2], 16 * (n // 2 + 1))
                    if n >= 2:
                        act.wait_ge(w_prod, NT * (n - 1))
                    a_(wh[:, n % 2], wraw[:, n % 2], ACT.Copy).then_inc(w_high, 1)
                    unit[0] += 1

            act.wait_ge(s_tm, 1)
            a_(t5b, PS[0:4, 6:8, :].rearrange("p b n -> p (b n)"), ACT.Copy).then_inc(s_tc, 1)
            act.wait_ge(s_lam, 1)
            a_(lam[:, 2:4], lam[:, 0:2], ACT.Exp).then_inc(s_lae, 1)
            for t in range(NT + 1):
                if t < NT:
                    act.wait_ge(s_x[t], 16)
                    if t > 0:
                        act.wait_ge(S("n1", "sq"), t)
                    a_(junk, xv[:, t, :], ACT.Square, accum_out=nss[:, t:t + 1]).then_inc(S("n1", "sq"), 1)
                if t > 0:
                    for q in range(2):
                        j = 2 * (t - 1) + q
                        act.wait_ge(S("n1", "tr"), j + 1)
                        a_(hTh[:, 4 * q:4 * q + 4, (t - 1) * P:t * P],
                           PS[:, j % 4, :].rearrange("p (k n) -> p k n", k=4), ACT.Copy).then_inc(S("n1", "high"), 1)
            split_units(2)
            act.wait_ge(S("n1", "high"), 2 * NT)
            act.sem_inc(s_pha, 1)

            def square(stage, j, src):
                if j >= 2:
                    act.wait_ge(S(stage, "ss"), j - 1)
                a_(sq[:, j % 2, :], src, ACT.Square).then_inc(S(stage, "sq"), 1)

            def evac_t(stage, jt, g0):
                c, t = divmod(jt, NT)
                act.wait_ge(S(stage, "tr"), jt + 1)
                a_((qT, kT)[c][:, :, t * P:(t + 1) * P], PS[:, 6 + jt % 2, :].rearrange("p (c n) -> p c n", c=4),
                   ACT.Copy, scale=gains[:, g0 + c:g0 + c + 1]).then_inc(S(stage, "tev"), 1)

            def project(stage, g0):
                chunks = [c for c in CHUNKS if c[0] == stage]
                jt = 0
                for c, (_, kind, u0, nu) in enumerate(chunks):
                    split_units(u0 + nu + 1)
                    for t in range(NT):
                        j = NT * c + t
                        if c < 2:
                            product_done(act, chunks[c], t)
                            square(stage, j, PS[:, t, :])
                        if jt <= j - 2 and jt < 2 * NT:
                            evac_t(stage, jt, g0)
                            jt += 1
                    while c == 1 and jt < 2 * NT:
                        evac_t(stage, jt, g0)
                        jt += 1
                    split_units(u0 + nu + 2)
                act.wait_ge(S(stage, "tev"), 2 * NT)
                act.sem_inc(s_pha, 1)

            def attend(br):
                L = ATT[br]
                nm = 2 if br == "diff" else 1
                for step in range(len(L) + 3):
                    a = step
                    if a < len(L):
                        n = L[a][3] * P
                        act.wait_ge(S(br, "biased"), a + 1)
                        for m in range(nm):
                            v = sT[:, a % 4, m, 0:n]
                            i = a_(v, v, ACT.Exp, bias=mx[:, a % 4, m:m + 1], scale=-1.0,
                                   accum_out=sm[:, a % 4, m:m + 1])
                        i.then_inc(S(br, "exp"), 1)
                    a = step - 1
                    if br == "diff" and 0 <= a < len(L):
                        n = L[a][3] * P
                        act.wait_ge(S(br, "ratio"), a + 1)
                        v = sT[:, a % 4, 1, 0:n]
                        a_(v, v, ACT.Copy, scale=ri[:, a % 8, 1:2]).then_inc(S(br, "second"), 1)
                    a = step - 3
                    if a >= 0:
                        n = L[a][3] * P
                        act.wait_ge(S(br, "tr"), a + 1)
                        if a >= 2:
                            act.wait_ge(S(br, "pv"), a - 1)
                        a_(aT[:, a % 2, 0:n], PS[:, 4 + a % 2, 0:n], ACT.Copy).then_inc(S(br, "aT"), 1)
                act.wait_ge(S(br, "aT"), len(L))
                act.sem_inc(s_pha, 1)

            project("pd", 0)
            attend("diff")
            act.wait_ge(S("diff", "out"), len(ATT["diff"]))
            for t in range(NT):
                square("yd", t, y_tok["diff"][:, t, :])
            act.wait_ge(S("yd", "ss"), NT)
            project("pn", 3)
            attend("na")

            def high_t(stage, jt, dst, signal, val, gain=None):
                act.wait_ge(signal, val)
                src = PS[:, 6 + jt % 2, :].rearrange("p (c n) -> p c n", c=4)
                i = a_(dst, src, ACT.Copy) if gain is None else a_(dst, src, ACT.Copy, scale=gain)
                i.then_inc(S(stage, "high"), 1)

            for t in range(NT):
                high_t("g", t, yTh[:, :, t * P:(t + 1) * P], S("g", "yd_t"), t + 1, gains[:, 2:3])
            chunks = [c for c in CHUNKS if c[0] == "g"]
            for c, (_, kind, u0, nu) in enumerate(chunks):
                if kind == "gate_n0":
                    for t in range(NT):
                        high_t("g", NT + t, yTh[:, :, t * P:(t + 1) * P], S("g", "yn_t"), t + 1)
                split_units(u0 + nu + 1)
                if kind[:4] == "gate":
                    half = int(kind[6])
                    for t in range(NT):
                        product_done(act, chunks[c], t)
                        if kind == "gate_n1":
                            act.wait_ge(S("g", "mul"), 2 * NT + t + 1)
                        dst = mm_[:, t, half * 512:(half + 1) * 512] if kind[5] == "d" else sg_n[:, t, :]
                        a_(dst, PS[:, t, :], ACT.Sigmoid).then_inc(S("g", "sig"), 1)
                split_units(u0 + nu + 2)
            act.wait_ge(S("g", "sig"), 4 * NT)
            act.sem_inc(s_pha, 1)
            for j in range(2 * NT):
                t, q = j % NT, j // NT
                high_t("o", j, hTh[:, 4 * q:4 * q + 4, t * P:(t + 1) * P], S("o", "m_t"), j + 1)
            split_units(UNITS - 2)
            split_units(UNITS - 1)
            split_units(UNITS)
            act.wait_ge(S("o", "high"), 2 * NT)
            act.sem_inc(s_pha, 1)
            for t in range(NT):
                act.wait_ge(S("o", "added"), NT + t + 1)
                if t > 0:
                    act.wait_ge(S("n2", "sq"), t)
                a_(junk2, xv[:, t, :], ACT.Square, accum_out=nss[:, t:t + 1]).then_inc(S("n2", "sq"), 1)
            for t in range(NT):
                for q in range(2):
                    j = 2 * t + q
                    act.wait_ge(S("n2", "tr"), j + 1)
                    if t >= 2:
                        act.wait_ge(S("rt", "logits"), t - 1)
                    a_(tT[:, t % 2, 4 * q:4 * q + 4, :], PS[:, j % 4, :].rearrange("p (k n) -> p k n", k=4),
                       ACT.Copy).then_inc(S("n2", "tev"), 1)
            act.wait_ge(S("rt", "shift"), 1)
            for t in range(NT):
                i = a_(aff[:, t, :], aff[:, t, :], ACT.Exp, bias=rmx[:, t:t + 1], accum_out=rsm[:, t:t + 1])
            i.then_inc(S("rt", "exp"), 1)
            act.wait_ge(S("rt", "exp"), 1)
            act.sem_inc(s_pha, 1)

            def misc_high(what, j, n, bank):
                act.wait_ge(S("x", "misc"), n)
                c0, w = (j * 4 * CAP, 4 * CAP) if what == "tokens" else (HR[j % 3][0] * CAP, HR[j % 3][1] * CAP)
                dst = xTh if what == "tokens" else hidh
                a_(dst[:, c0:c0 + w], PS[:, bank, 0:w], ACT.Copy).then_inc(S("x", "misc_high"), 1)

            for q in range(PRE):
                misc_high("tokens", q, q + 1, 6 + q)
            with act.Fori(0, E) as e:
                for w in range(NXU + 2):
                    if w < NXU:
                        act.wait_ge(x_loaded[w % RAWS], e * 16 * (NXU // RAWS) + 16 * (w // RAWS + 1))
                        act.wait_ge(x_used, e * NXU + w + 1)
                        n = unit_width(w)
                        a_(xh[:, w % SPLITS, 0:n], xraw[:, w % RAWS, 0:n], ACT.Copy).then_inc(x_high, 1)
                    if w == 2:
                        act.wait_ge(S("x", "cur"), e + 1)
                        for half in range(2):
                            i = a_(yeh[:, half * 512:(half + 1) * 512], PS[0:CAP, 4 + half, :], ACT.Copy,
                                   scale=cur_g)
                        i.then_inc(S("x", "ye_high"), 1)
                    u = w - 2
                    if 0 <= u < NXU:
                        kind, q, c = XU[u]
                        if kind == "gate" and c == 1:
                            act.wait_ge(x_used, e * NXU + u + 1 + SPLITS)
                            if q > 0:
                                act.wait_ge(S("x", "hidden"), e * 4 + q)
                            a_(sg.rearrange("p (h f) -> p h f", h=2), PS[0:CAP, 0:2, 0:QC], ACT.Silu
                               ).then_inc(S("x", "silu"), 1)
                        for what, j in MISC.get(u, []):
                            if what != "scatter":
                                n = use_no(what, j)
                                misc_high(what, j, e * NU + PRE + n + 1, 6 + n % 2)
            act.wait_ge(S("x", "cur"), E + 1)
            act.wait_ge(x_used, NXU * E + SPLITS)
            for half in range(2):
                i = a_(yeh[:, half * 512:(half + 1) * 512], PS[0:CAP, 4 + half, :], ACT.Copy, scale=cur_g)
            i.then_inc(S("x", "ye_high"), 1)

        @block.vector
        def _(dve):
            v = nc.vector

            def link(ins):
                chain_count[0] += 1
                ins.then_inc(s_dv, 1)
                dve.wait_ge(s_dv, chain_count[0])

            unit = [0]

            def low(out, src, high):
                return v.tensor_tensor(out, src, high.bitcast(F32), ALU.subtract)

            def split_units(upto):
                while unit[0] < min(upto, UNITS):
                    n = unit[0]
                    dve.wait_ge(w_high, n + 1)
                    low(wl[:, n % 2], wraw[:, n % 2], wh[:, n % 2]).then_inc(w_split, 1)
                    unit[0] += 1

            dve.sem_inc(x_split, RAWS)
            dve.wait_ge(s_lamv, 16 * 13)
            for m in range(2):
                i = v.tensor_tensor(lamv[:, 2 * m, :], lamv[:, 2 * m, :], lamv[:, 2 * m + 1, :], ALU.mult)
            link(i)
            for m in range(2):
                i = v.tensor_reduce(lam[:, m:m + 1], lamv[:, 2 * m, :], AX.X, ALU.add)
            i.then_inc(s_lam, 1)
            dve.wait_ge(s_lam, 1)
            for c, s_ in ((0, 0.125), (2, 1.0 - LAM0), (3, 0.125)):
                i = v.tensor_scalar(gains[:, c:c + 1], gains[:, c:c + 1], s_, None, ALU.mult)
            dve.wait_ge(s_lae, 1)
            link(v.scalar_tensor_tensor(lam[:, 0:1], lam[:, 2:3], LAM0, lam[:, 3:4], ALU.add, ALU.subtract))
            dve.wait_ge(s_cst, 32)

            def mean_eps(out, in_, w, done):
                return v.tensor_scalar(out, in_, 1.0 / w, EPS, ALU.mult, ALU.add).then_inc(done, 1)

            def norm_tokens(stage, gb, dst, bufs_free, then):
                for t in range(NT + 2):
                    if t < NT:
                        dve.wait_ge(S(stage, "sq"), t + 1)
                        mean_eps(nss[:, t:t + 1], nss[:, t:t + 1], D, S(stage, "ss"))
                    if 0 < t <= NT:
                        u = t - 1
                        dve.wait_ge(S(stage, "rs"), u + 1)
                        bufs_free(u)
                        v.scalar_tensor_tensor(dst[:, u % 2, :], xv[:, u, :], nrs[:, u:u + 1], gb, ALU.mult,
                                               ALU.mult).then_inc(S(stage, "hn"), 1)
                    if t > 1:
                        then(t - 2)

            def hn_free(u):
                if u >= 2:
                    dve.wait_ge(S("n1", "tr"), 2 * (u - 1))

            def hT_low(t):
                for q in range(2):
                    j = 2 * t + q
                    dve.wait_ge(S("n1", "high"), j + 1)
                    dst = (slice(None), slice(4 * q, 4 * q + 4), slice(t * P, (t + 1) * P))
                    low(hTl[dst], PS[:, j % 4, :].rearrange("p (k n) -> p k n", k=4), hTh[dst]
                        ).then_inc(S("n1", "tev"), 1)

            norm_tokens("n1", g1b, hn, hn_free, hT_low)
            split_units(2)
            dve.wait_ge(S("n1", "tev"), 2 * NT)
            dve.sem_inc(s_phd, 1)

            def reduce_sq(stage, j, heads, hd):
                dve.wait_ge(S(stage, "sq"), j + 1)
                if j >= 4:
                    dve.wait_ge(S(stage, "qn"), j - 3)
                link(v.tensor_reduce(ss[:, j % 4, 0:heads], sq[:, j % 2, :].rearrange("p (h d) -> p h d", h=heads),
                                     AX.X, ALU.add))
                mean_eps(ss[:, j % 4, 0:heads], ss[:, j % 4, 0:heads], hd, S(stage, "ss"))

            def scale_q(stage, j, dst, src, heads, hd):
                dve.wait_ge(S(stage, "rs"), j + 1)
                r = rs[:, j % 4, 0:heads].unsqueeze(2).to_broadcast((P, heads, hd))
                return v.tensor_tensor(dst.rearrange("p (h d) -> p h d", h=heads),
                                       src.rearrange("p (h d) -> p h d", h=heads), r, ALU.mult
                                       ).then_inc(S(stage, "qn"), 1)

            def scale_proj(stage, j):
                if j >= 2:
                    dve.wait_ge(S(stage, "tr"), j - 1)
                scale_q(stage, j, qn[:, j % 2, :], PS[:, j % NT, :], 8, 64)
                dve.wait_ge(S(stage, "qn"), j + 1)
                dve.sem_inc(S(stage, "pused"), 1)

            def project(stage):
                chunks = [c for c in CHUNKS if c[0] == stage]
                for c, (_, kind, u0, nu) in enumerate(chunks):
                    split_units(u0 + nu + 1)
                    for t in range(NT):
                        j = NT * c + t
                        if c < 2:
                            reduce_sq(stage, j, 8, 64)
                            if t > 0:
                                scale_proj(stage, j - 1)
                        else:
                            product_done(dve, chunks[c], t)
                            v.tensor_copy(vv[:, t, :], PS[:, t, :]).then_inc(S(stage, "pused"), 1)
                    if c < 2:
                        scale_proj(stage, NT * c + NT - 1)
                    split_units(u0 + nu + 2)
                dve.wait_ge(S(stage, "pused"), 3 * NT)
                dve.sem_inc(s_phd, 1)

            def attend(br):
                L = ATT[br]
                nm = 2 if br == "diff" else 1
                for step in range(len(L) + 4):
                    a = step
                    if a < len(L):
                        h, qt, t0, nt = L[a]
                        n = nt * P
                        nh = h if br == "diff" else 4 + h
                        b = nh % 2
                        if a % HPI == 0:
                            if br == "diff":
                                dve.wait_ge(s_b[b], 16 * (h // 2 + 1))
                            else:
                                dve.wait_ge(s_bm, h + 1)
                        dve.wait_ge(S(br, "log"), a + 1)
                        if a >= 4:
                            dve.wait_ge(S(br, "tr"), a - 3)
                        c0 = 384 - 128 * qt
                        for m in range(nm):
                            i = v.tensor_tensor_reduce(
                                out=sT[:, a % 4, m, 0:n], in0=PS[:, 2 * (a % 2) + m, 0:n], in1=bias[:, b, c0:c0 + n],
                                scale=-1.0, scalar=3.0e38, op0=ALU.add, op1=ALU.min,
                                accum_out=mx[:, a % 4, m:m + 1])
                        i.then_inc(S(br, "biased"), 1)
                    a = step - 1
                    if 0 <= a < len(L):
                        n = L[a][3] * P
                        dve.wait_ge(S(br, "exp"), a + 1)
                        if br == "diff":
                            link(v.reciprocal(ri[:, a % 8, :], sm[:, a % 4, :]))
                            v.tensor_tensor(ri[:, a % 8, 1:2], ri[:, a % 8, 1:2], lam[:, 0:1], ALU.mult
                                            ).then_inc(S(br, "ratio"), 1)
                        else:
                            v.reciprocal(ri[:, a % 8, 0:1], sm[:, a % 4, 0:1]).then_inc(S(br, "probs"), 1)
                    a = step - 2
                    if br == "diff" and 0 <= a < len(L):
                        n = L[a][3] * P
                        dve.wait_ge(S(br, "second"), a + 1)
                        v.scalar_tensor_tensor(sT[:, a % 4, 0, 0:n], sT[:, a % 4, 0, 0:n], ri[:, a % 8, 0:1],
                                               sT[:, a % 4, 1, 0:n], ALU.mult, ALU.subtract
                                               ).then_inc(S(br, "probs"), 1)
                    a = step - 4
                    if 0 <= a < len(L):
                        h, qt, t0, nt = L[a]
                        dve.wait_ge(S(br, "pv"), a + 1)
                        w = P if br == "diff" else 64
                        dst = y_tok[br][:, t0 + qt, h * w:(h + 1) * w]
                        if br == "diff":
                            i = v.tensor_copy(dst, PS[:, 6 + a % 2, 0:w])
                        else:
                            i = v.tensor_scalar(dst, PS[:, 6 + a % 2, 0:w], ri[:, a % 8, 0:1], None, ALU.mult)
                        i.then_inc(S(br, "out"), 1)
                dve.wait_ge(S(br, "out"), len(L))
                dve.sem_inc(s_phd, 1)

            project("pd")
            attend("diff")
            for t in range(NT + 1):
                if t < NT:
                    reduce_sq("yd", t, 4, 128)
                if t > 0:
                    y = y_tok["diff"][:, t - 1, :]
                    scale_q("yd", t - 1, y, y, 4, 128)
            project("pn")
            attend("na")

            def low_t(stage, jt, dl, dh, gain=None):
                dve.wait_ge(S(stage, "high"), jt + 1)
                src = PS[:, 6 + jt % 2, :].rearrange("p (c n) -> p c n", c=4)
                if gain is None:
                    i = low(dl, src, dh)
                else:
                    dl2, dh2 = dl, dh.bitcast(F32)
                    i = v.scalar_tensor_tensor(dl2, src, gain, dh2, ALU.mult, ALU.subtract)
                i.then_inc(S(stage, "tev"), 1)

            for t in range(NT):
                cols = slice(t * P, (t + 1) * P)
                low_t("g", t, yTl[:, :, cols], yTh[:, :, cols], gains[:, 2:3])
            chunks = [c for c in CHUNKS if c[0] == "g"]
            for c, (_, kind, u0, nu) in enumerate(chunks):
                if kind == "gate_n0":
                    for t in range(NT):
                        cols = slice(t * P, (t + 1) * P)
                        low_t("g", NT + t, yTl[:, :, cols], yTh[:, :, cols])
                split_units(u0 + nu + 1)
                if kind[:2] == "br":
                    half = int(kind[4])
                    for t in range(NT):
                        product_done(dve, chunks[c], t)
                        dve.wait_ge(S("g", "sig"), NT * (c // 2) + t + 1)
                        m = mm_[:, t, half * 512:(half + 1) * 512]
                        if kind[3] == "d":
                            v.tensor_tensor(m, m, PS[:, t, :], ALU.mult).then_inc(S("g", "mul"), 1)
                        else:
                            g = sg_n[:, t, :]
                            link(v.tensor_tensor(g, g, PS[:, t, :], ALU.mult))
                            v.tensor_tensor(m, m, g, ALU.add).then_inc(S("g", "mul"), 1)
                split_units(u0 + nu + 2)
            dve.wait_ge(S("g", "mul"), 4 * NT)
            dve.sem_inc(s_phd, 1)
            for j in range(2 * NT):
                t, q = j % NT, j // NT
                dst = (slice(None), slice(4 * q, 4 * q + 4), slice(t * P, (t + 1) * P))
                low_t("o", j, hTl[dst], hTh[dst])
            split_units(UNITS - 2)
            split_units(UNITS - 1)
            for c in range(2):
                if c == 1:
                    split_units(UNITS)
                for t in range(NT):
                    product_done(dve, CHUNKS[len(CHUNKS) - 2 + c], t)
                    if c == 0:
                        dve.wait_ge(s_x[t], 32)
                    xs = xv[:, t, c * 512:(c + 1) * 512]
                    v.tensor_tensor(xs, xs, PS[:, t, :], ALU.add).then_inc(S("o", "added"), 1)
            dve.wait_ge(S("o", "added"), 2 * NT)
            dve.sem_inc(s_phd, 1)
            dve.wait_ge(S("rt", "g2"), 16)

            def tn_free(u):
                if u >= 2:
                    dve.wait_ge(S("n2", "tr"), 2 * (u - 1))
                    dve.wait_ge(S("n2", f"stored{u % 2}"), 16 * (u // 2))

            norm_tokens("n2", g2b, tn, tn_free, lambda t: None)
            dve.wait_ge(S("rt", "logits"), NT)
            lg = PS[:, 4, 0:NT * E].rearrange("p (t e) -> p t e", t=NT)
            v.tensor_copy(aff, lg)
            v.tensor_reduce(rmx, lg, AX.X, ALU.max, negate=True).then_inc(S("rt", "shift"), 1)
            dve.wait_ge(S("rt", "exp"), 1)
            link(v.reciprocal(rrs, rsm))
            v.tensor_tensor(aff, aff, rrs.unsqueeze(2).to_broadcast((P, NT, E)), ALU.mult).then_inc(S("rt", "aff"), 1)
            dve.wait_ge(S("rt", "aff"), 1)
            v.tensor_copy(R[:, :, :, 1], aff)
            v.tensor_copy(R[:, :, :, 0], tokid.unsqueeze(2).to_broadcast((P, NT, E)))
            v.memset(ones, 1.0)
            dve.wait_ge(S("rt", "affT"), 1)
            link(v.tensor_copy(affT[:, 0:512], PS[0:E, 5, :]))
            link(v.tensor_copy(affT[:, 512:768], PS[0:E, 6, 0:256]))
            link(v.tensor_copy(work, affT))
            for lo, hi, cap in ((0, SP_, CP), (SP_, N, CS)):
                for r in range(cap // 8):
                    link(v.max(m8, work[:, lo:hi]))
                    link(v.match_replace(work[:, lo:hi], m8, work[:, lo:hi], -1.0))
            link(v.tensor_tensor(selT, affT, work, ALU.not_equal))
            for lo, hi in ((0, SP_), (SP_, N)):
                link(v.tensor_tensor_scan(cumT[:, lo:hi], ones[:, 0:hi - lo], selT[:, lo:hi], 0.0, ALU.mult, ALU.add))
            v.tensor_tensor(cumT, cumT, selT, ALU.mult).then_inc(S("rt", "rank"), 1)
            dve.wait_ge(S("rt", "rkT"), 1)
            link(v.tensor_copy(rk, PS[:, 7, 0:NT * E].rearrange("p (t e) -> p t e", t=NT)))
            for t in range(NT):
                w = CS if t >= 2 else CP
                if t >= 2:
                    dve.wait_ge(S("rt", "slots"), t - 1)
                v.tensor_tensor(G[:, t % 2, :, 0:w], rk[:, t, :].unsqueeze(2).to_broadcast((P, E, w)),
                                slot1[:, 0:w].unsqueeze(1).to_broadcast((P, E, w)), ALU.is_equal
                                ).then_inc(S("rt", "G"), 1)
            v.memset(idxf[:, 0:1], -1.0)
            v.memset(gate_s[:, 0:1], 0.0)
            link(v.memset(idxi[:, 0:1], 0))
            dve.wait_ge(S("rt", "slots"), NT)
            for p0, w, b in ((0, CS, 1), (CS, CP, 0)):
                tab = PS[p0:p0 + w, b, 0:2 * E].rearrange("p (e c) -> p e c", c=2)
                v.tensor_copy(idxf[p0:p0 + w, 1:E + 1], tab[:, :, 0])
                i = v.tensor_copy(gate_s[p0:p0 + w, 1:E + 1], tab[:, :, 1])
            link(i)
            v.tensor_copy(idxi[:, 1:E + 1], idxf[:, 1:E + 1]).then_inc(S("rt", "tables"), 1)
            for half in range(2):
                i = v.memset(PS[0:CAP, 4 + half, :], 0.0)
            link(i)
            dve.sem_inc(s_phd, 1)

            def misc_low(what, j, n, n_high, bank):
                dve.wait_ge(S("x", "misc_high"), n_high)
                c0, w = (j * 4 * CAP, 4 * CAP) if what == "tokens" else (HR[j % 3][0] * CAP, HR[j % 3][1] * CAP)
                dh, dl = (xTh, xTl) if what == "tokens" else (hidh, hidl)
                low(dl[:, c0:c0 + w], PS[:, bank, 0:w], dh[:, c0:c0 + w]).then_inc(S("x", "misc_read"), 1)

            def slot_tables(e, val):
                v.tensor_copy(cur_f, idxf[:, bass.ds(e, 1)])
                v.tensor_copy(cur_g, gate_s[:, bass.ds(e, 1)]).then_inc(S("x", "cur"), 1)
                dve.wait_ge(S("x", "cur"), val)
                v.tensor_scalar(scat, iota_tok, cur_f, None, ALU.is_equal).then_inc(S("x", "onehot"), 1)

            def result_low(val):
                dve.wait_ge(S("x", "ye_high"), val)
                for half in range(2):
                    cols = slice(half * 512, (half + 1) * 512)
                    i = v.scalar_tensor_tensor(yel[:, cols], PS[0:CAP, 4 + half, :], cur_g,
                                               yeh[:, cols].bitcast(F32), ALU.mult, ALU.subtract)
                i.then_inc(S("x", "ye_low"), 1)

            dve.wait_ge(S("x", "iota"), 1)
            for q in range(PRE):
                misc_low("tokens", q, q + 1, q + 1, 6 + q)
            highs = [m for _, m in USES if m[0] != "scatter"]
            with dve.Fori(0, E) as e:
                slot_tables(e, e + 1)
                for w in range(NXU + 2):
                    if w < NXU:
                        n = unit_width(w)
                        dve.wait_ge(x_high, e * NXU + w + 1)
                        low(xl[:, w % SPLITS, 0:n], xraw[:, w % RAWS, 0:n], xh[:, w % SPLITS, 0:n]
                            ).then_inc(x_split, 1)
                    if w == 2:
                        result_low(e + 1)
                    u = w - 2
                    if 0 <= u < NXU:
                        kind, q, c = XU[u]
                        if kind == "up" and c == 1:
                            dve.wait_ge(x_used, e * NXU + u + 1 + SPLITS)
                            dve.wait_ge(S("x", "silu"), e * 4 + q + 1)
                            h0 = (q % 2) * QF
                            v.tensor_tensor(hid[:, h0:h0 + QF].rearrange("p (h f) -> p h f", h=2),
                                            sg.rearrange("p (h f) -> p h f", h=2), PS[0:CAP, 2:4, 0:QC], ALU.mult
                                            ).then_inc(S("x", "hidden"), 1)
                        for what, j in MISC.get(u, []):
                            n = use_no(what, j)
                            if what == "scatter":
                                t, half = divmod(j, 2)
                                dve.wait_ge(S("x", "misc"), e * NU + PRE + n + 1)
                                xs = xv[:, t, half * 512:(half + 1) * 512]
                                v.tensor_tensor(xs, xs, PS[:, 6 + n % 2, :], ALU.add).then_inc(S("x", "misc_read"), 1)
                            else:
                                misc_low(what, j, e * NU + PRE + n + 1, e * NH_ + PRE + highs.index((what, j)) + 1,
                                         6 + n % 2)
            slot_tables(E, E + 1)
            result_low(E + 1)
            for j in range(12):
                t, half = divmod(j, 2)
                dve.wait_ge(S("x", "misc"), E * NU + PRE + j + 1)
                xs = xv[:, t, half * 512:(half + 1) * 512]
                i = v.tensor_tensor(xs, xs, PS[:, 6 + j % 2, :], ALU.add)
                i.then_inc(S("x", "misc_read"), 1)
                dve.wait_ge(S("x", "misc_read"), E * NU + PRE + j + 1)
                dve.sem_inc(S("x", "last_added"), 1)


_INS = ["x_prompt", "x_sample", "norm1_g", "w_in", "diff_q_norm", "diff_k_norm", "lambda_q1", "lambda_k1",
        "lambda_q2", "lambda_k2", "diff_subln_g", "rel_bias", "na_q_norm", "na_k_norm", "na_rpb", "w_branch_diff",
        "w_branch_na", "w_out", "norm2_g", "w_router", "w_expert_gate", "w_expert_up", "w_expert_down"]
_KEEP2D = {"norm1_g", "norm2_g", "diff_q_norm", "diff_k_norm", "lambda_q1", "lambda_k1", "lambda_q2", "lambda_k2",
           "diff_subln_g", "rel_bias", "na_q_norm", "na_k_norm"}


def _constants():
    import numpy as np
    c = np.zeros((P, C_W), np.float32)
    c[:, C_ID:C_ID + 128] = np.eye(P)
    col = np.arange(P) % 64
    start = np.clip(col - 8, 0, 48)[:, None]
    kc = np.arange(64)[None, :]
    c[:, C_MASK:C_MASK + 64] = np.where((kc >= start) & (kc < start + 16), 0.0, -1e30)
    c[:, C_TOK:C_TOK + NT] = np.arange(NT)[None, :] * P + np.arange(P)[:, None]
    c[:, C_SLOT:C_SLOT + 64] = 1 + np.arange(64)
    c[:, C_POW:C_POW + 64] = -0.5
    rel = np.arange(1024) - 511
    n = np.abs(rel)
    f = np.float32
    large = 8 + (np.log(np.maximum(n, 1).astype(f) / f(8)) / f(math.log(16.0)) * f(8)).astype(np.int32)
    bucket = np.where(rel > 0, 16, 0) + np.where(n < 8, n, np.minimum(large, 15))
    onehot = (np.arange(32)[:, None] == bucket[None, :]).astype(f)
    return c, onehot


def kernel(**inputs):
    import numpy as np
    import concourse.bacc as bacc
    from concourse.bass_utils import run_bass_kernel_spmd

    nc = bacc.Bacc("TRN2", target_bir_lowering=False, num_devices=1)
    arrays, args = {}, []

    def give(name, a):
        arrays[name] = a
        args.append(nc.dram_tensor(name, a.shape, mybir.dt.from_np(a.dtype), kind="ExternalInput").ap())

    for name in _INS:
        a = np.ascontiguousarray(inputs[name])
        give(f"in_{name}", a if name in _KEEP2D else a.reshape(a.shape[1:]))
    cst, onehot = _constants()
    give("in_consts", cst)
    give("in_t5_onehot", onehot)
    args.append(nc.dram_tensor("out_prompt", (SP_, D), F32, kind="ExternalOutput").ap())
    args.append(nc.dram_tensor("out_sample", (SS, D), F32, kind="ExternalOutput").ap())
    encoder(nc, *args)
    r = run_bass_kernel_spmd(nc, [arrays], core_ids=[0])
    out = r.results[0]
    return out["out_prompt"].reshape(1, SP_, D), out["out_sample"].reshape(1, SS, D)
```

```python
import math
from contextlib import ExitStack

import concourse.bass as bass
from concourse import mybir

P = 128
D = 1024
SP_, SS = 256, 512
N = SP_ + SS
NT = N // P
KD = D // P
HW = 512
FF = 2816
E = 16
HF = FF // 2
QF = FF // 4
QC = QF // 2
FT = HF // P
CP, CS = 2 * SP_ // E, 2 * SS // E
CAP = CP + CS
EPS = 1e-6
LAM0 = 0.8 - 0.6 * math.exp(0.0)
BW = 896
NA_ROWS = 15
GROUPS = [(0, 2), (2, 4)]

F32 = mybir.dt.float32
F32R = mybir.dt.float32r
I32 = mybir.dt.int32
BF16 = mybir.dt.bfloat16
ALU = mybir.AluOpType
ACT = mybir.ActivationFunctionType
AX = mybir.AxisListType

C_ID, C_MASK, C_TOK, C_SLOT, C_POW = 0, 128, 192, 198, 262
C_W = C_POW + 64

UNIT = 4 * 512
CHUNKS = []
for _stage, _kinds in (("pd", ("q", "k", "v")), ("pn", ("q", "k", "v")),
                       ("g", ("gate_d0", "br_d0", "gate_d1", "br_d1", "gate_n0", "br_n0", "gate_n1", "br_n1")),
                       ("o", ("out0", "out1"))):
    for _kind in _kinds:
        _at = CHUNKS[-1][2] + CHUNKS[-1][3] if CHUNKS else 0
        CHUNKS.append((_stage, _kind, _at, 1 if _kind[:2] == "br" else 2))
UNITS = CHUNKS[-1][2] + CHUNKS[-1][3]

OUT_ORDER = [(0, 0), (1, 0), (0, 1), (1, 1)] + [(_t, _c) for _t in range(2, NT) for _c in range(2)]
START_EARLY = 5

XU = []
for _q in range(4):
    XU += [("gate", _q, 0), ("gate", _q, 1)]
    if _q == 2:
        XU += [("down", 0, _c) for _c in range(4)]
    XU += [("up", _q, 0), ("up", _q, 1)]
XU += [("down", 1, _c) for _c in range(4)]
NXU = len(XU)
XUNIT = 3 * D
DT = [(0, 2), (2, 3), (5, 3), (8, 3)]
HR = [(0, 5), (5, 3), (8, 3)]
RAWS, SPLITS = 4, 3


def after(kind, part, c=1):
    return XU.index((kind, part, c))


MISC = {after("gate", 1): [("hidden", 0)], after("gate", 2, 0): [("hidden", 1)], after("gate", 2): [("hidden", 2)],
        after("gate", 3, 0): [("hidden", 3)], after("up", 3): [("tokens", 0)],
        after("down", 1, 0): [("hidden", 4)], after("down", 1, 1): [("hidden", 5), ("tokens", 1)]}
for _j, _w in enumerate([_w for _w in range(2, NXU) if _w not in MISC][:12]):
    MISC[_w] = [("scatter", _j)]
USES = [(w, m) for w in sorted(MISC) for m in MISC[w]]
NU = len(USES)
PRE = 2
NH_ = sum(m[0] != "scatter" for _, m in USES)


def use_no(kind, i):
    return [m for _, m in USES].index((kind, i))


def encoder(nc, x_prompt, x_sample, norm1_g, w_in, diff_q_norm, diff_k_norm, lambda_q1, lambda_k1, lambda_q2,
            lambda_k2, diff_subln_g, rel_bias, na_q_norm, na_k_norm, na_rpb, w_branch_diff, w_branch_na, w_out,
            norm2_g, w_router, w_expert_gate, w_expert_up, w_expert_down, consts, t5_onehot, y_prompt, y_sample):
    ctx = ExitStack()
    with ctx:
        BASE = -(-nc.sbuf_base // 64) * 64

        def at(name, off, cols, parts=P, dt=F32):
            return nc.alloc_sbuf_tensor_at(name, [parts, cols], dt, offset=BASE + 4 * off)[:, :]

        def sem(name):
            return ctx.enter_context(nc.semaphore(name))

        cst = at("cst", 0, C_W)
        small = at("small", 328, 400)
        wrt_v = at("wrt", 728, KD * E).rearrange("p (k e) -> p k e", k=KD)
        idxf = at("idxf", 856, E + 1, CAP)
        gate_s = at("gate_s", 880, E + 1, CAP)
        idxi = at("idxi", 904, E + 1, CAP, I32)
        cur_f = at("cur_f", 928, 1, CAP)
        cur_g = at("cur_g", 936, 1, CAP)
        xv = at("x", 960, NT * D).rearrange("p (t d) -> p t d", t=NT)
        y_tok = {"diff": at("yd", 960, NT * HW).rearrange("p (t n) -> p t n", t=NT),
                 "na": at("yn", 960 + 3072, NT * HW).rearrange("p (t n) -> p t n", t=NT)}
        hTh = at("hT_high", 7104, 6144, dt=F32R).rearrange("p (k n) -> p k n", k=KD)
        hTl = at("hT_low", 13248, 6144, dt=F32R).rearrange("p (k n) -> p k n", k=KD)
        wraw = at("w_raw", 19392, 2 * UNIT).rearrange("p (b k n) -> p b k n", b=2, k=4)
        wh = at("w_high", 23488, 2 * UNIT, dt=F32R).rearrange("p (b k n) -> p b k n", b=2, k=4)
        wl = at("w_low", 27584, 2 * UNIT, dt=F32R).rearrange("p (b k n) -> p b k n", b=2, k=4)
        qT = at("qT", 31680, 3072).rearrange("p (c n) -> p c n", c=4)
        kT = [at(f"kT{r}", off, 3072).rearrange("p (c n) -> p c n", c=4) for r, off in enumerate((34752, 49280))]
        vv = at("v", 37824, 3072).rearrange("p (t n) -> p t n", t=NT)
        sT = at("s", 40896, 4096).rearrange("p (b m n) -> p b m n", b=4, m=2)
        sq = at("sq", 40896, 1024).rearrange("p (b n) -> p b n", b=2)
        qn = at("qn", 41920, 1024).rearrange("p (b n) -> p b n", b=2)
        bias = at("bias", 44992, 2 * BW).rearrange("p (b n) -> p b n", b=2)
        aT = at("aT", 46784, 1024).rearrange("p (b n) -> p b n", b=2)
        hn = at("hn", 31680, 2048).rearrange("p (b n) -> p b n", b=2)
        junk = at("junk", 33728, 1024)
        g1b = at("g1b", 37824, 1024)
        t5b = at("t5b", 44992, 1024, 4)
        t5t = at("t5t", 47808, 4, 32)
        napad = at("napad", 47872, 128, 120)
        t5h = at("t5h", 48000, 1024, 32)
        lamv = at("lamv", 49024, 256).rearrange("p (v d) -> p v d", v=4)
        yTh = at("yT_high", 31680, 3072, dt=F32R).rearrange("p (c n) -> p c n", c=4)
        yTl = at("yT_low", 34752, 3072, dt=F32R).rearrange("p (c n) -> p c n", c=4)
        mm_ = at("merged", 37824, NT * D).rearrange("p (t n) -> p t n", t=NT)
        sg_n = at("sig_na", 43968, NT * HW).rearrange("p (t n) -> p t n", t=NT)
        wh_o = at("w_high_out1", 43968, 2 * UNIT, dt=F32R).rearrange("p (b k n) -> p b k n", b=2, k=4)
        wl_o = at("w_low_out1", 48064, 2 * UNIT, dt=F32R).rearrange("p (b k n) -> p b k n", b=2, k=4)
        tn = at("tn", 19392, 2048).rearrange("p (b n) -> p b n", b=2)
        tT = at("tT", 21440, 2048).rearrange("p (b k n) -> p b k n", b=2, k=KD)
        g2b = at("g2b", 40896, 1024)
        G = at("G", 27072, 4 * E * 64, dt=BF16).rearrange("p (b e s) -> p b e s", b=4, e=E)
        rk = at("rk", 29120, 96).rearrange("p (t e) -> p t e", t=NT)
        R = at("R", 29216, 192).rearrange("p (t e c) -> p t e c", t=NT, c=2)
        R3 = at("R_parts", 29408, 576, dt=BF16).rearrange("p (t e m c) -> p t e m c", t=NT, e=E, m=3)
        affT = at("affT", 48704, 768, E)
        work = at("work", 49472, 768, E)
        selT = at("selT", 50240, 768, E)
        cumT = at("cumT", 51008, 768, E)
        ones = at("ones", 51776, 512, E)
        xl = at("x_w_low", 7104, SPLITS * XUNIT, dt=F32R).rearrange("p (b n) -> p b n", b=SPLITS)
        xh = at("x_w_high", 16320, SPLITS * XUNIT, dt=F32R).rearrange("p (b n) -> p b n", b=SPLITS)
        xTh = at("xT_high", 25536, KD * CAP, dt=F32R)
        xTl = at("xT_low", 26304, KD * CAP, dt=F32R)
        hidh = at("hidden_high", 27072, FT * CAP, dt=F32R)
        hidl = at("hidden_low", 28128, FT * CAP, dt=F32R)
        yeh = at("y_high", 29184, D, CAP, dt=F32R)
        yel = at("y_low", 30208, D, CAP, dt=F32R)
        xraw = at("x_w_raw", 31680, RAWS * XUNIT).rearrange("p (b n) -> p b n", b=RAWS)
        scat = at("scatter_onehot", 43968, N, CAP, dt=F32R)
        xe = at("gathered", 44736, D, CAP)
        hid = at("hidden", 45760, HF, CAP)
        sg = at("silu", 47168, QF, CAP)
        iota_tok = at("iota_tok", 47872, N, CAP)

        ident = cst[:, C_ID:C_ID + 128]
        mask = cst[:, C_MASK:C_MASK + 64]
        tokid = cst[:, C_TOK:C_TOK + NT]
        slot1 = cst[:, C_SLOT:C_SLOT + 64]
        mhalf = cst[:, C_POW:C_POW + 64]

        ss = small[:, 0:32].rearrange("p (b n) -> p b n", b=4)
        rs = small[:, 32:64].rearrange("p (b n) -> p b n", b=4)
        nss = small[:, 64:70]
        nrs = small[:, 72:78]
        mx = small[:, 80:88].rearrange("p (b m) -> p b m", b=4)
        sm = small[:, 88:96].rearrange("p (b m) -> p b m", b=4)
        ri = small[:, 96:112].rearrange("p (b m) -> p b m", b=8)
        lam = small[:, 112:116]
        gains = small[:, 120:128]
        rmx = small[:, 128:134]
        rsm = small[:, 136:142]
        rrs = small[:, 144:150]
        m8 = small[0:E, 152:160]
        aff = small[:, 200:296].rearrange("p (t e) -> p t e", t=NT)

        PS = ctx.enter_context(nc.psum_tensor("PS", [P, 8, 512], F32))
        t5_dram = nc.dram_tensor("t5_dram", [4, 1024], F32, kind="Internal").ap()
        na_dram = nc.dram_tensor("na_dram", [120, 128], F32, kind="Internal").ap()
        t5_rep = nc.dram_tensor("t5_rep", [4, P, 1024], F32, kind="Internal").ap()
        na_rep = nc.dram_tensor("na_rep", [8, 64, NA_ROWS * 128], F32, kind="Internal").ap()
        t_dram = nc.dram_tensor("t_dram", [N, D], F32, kind="Internal").ap()

        s_x = [sem(f"x_loaded{t}") for t in range(NT)]
        s_cst = sem("constants_loaded")
        s_lamv = sem("lambdas_loaded")
        s_tab = sem("tables_loaded")
        s_nz = sem("na_pad_zeroed")
        s_kz = sem("keys_zeroed")
        s_nt = sem("na_table_in_pad")
        s_tm = sem("t5_rows_ready")
        s_tc = sem("t5_rows_in_sbuf")
        s_scr = sem("bias_rows_in_dram")
        s_rep = sem("bias_rows_replicated")
        s_b = [sem(f"bias_loaded{b}") for b in range(2)]
        s_bm = sem("bias_masked")
        s_pha = sem("act_done_with_stage")
        s_phd = sem("dve_done_with_stage")
        s_dv = sem("dve_chain")
        s_lam = sem("lambda_sums_ready")
        s_lae = sem("lambda_exps_ready")
        w_loaded = [sem(f"unit_loaded{b}") for b in range(2)]
        w_high = sem("unit_high_ready")
        w_split = sem("unit_split_ready")
        w_prod = sem("unit_tile_products")
        x_loaded = [sem(f"x_unit_loaded{b}") for b in range(RAWS)]
        x_high = sem("x_unit_high_ready")
        x_split = sem("x_unit_split_ready")
        x_used = sem("x_unit_used")

        sems = {}

        def S(stage, name):
            k = f"{stage}_{name}"
            if k not in sems:
                sems[k] = sem(k)
            return sems[k]

        chain_count = [0]

        def xsrc(a, b, t):
            return a[t * P:(t + 1) * P, :] if t < 2 else b[(t - 2) * P:(t - 1) * P, :]

        def items(heads):
            return [(h, qt, t0, nt) for h in range(heads) for (t0, nt) in GROUPS for qt in range(nt)]

        ATT = {"diff": items(4), "na": items(8)}
        HPI = NT

        def stage_done(eng, k):
            eng.wait_ge(s_pha, k)
            eng.wait_ge(s_phd, k)

        def product_done(eng, chunk, t):
            eng.wait_ge(w_prod, NT * (chunk[2] + chunk[3] - 1) + t + 1)

        OUT = UNITS - 4

        def out_done(eng, t, c):
            eng.wait_ge(w_prod, NT * OUT + 2 * OUT_ORDER.index((t, c)) + 2)

        def split_slot(n):
            return (wh_o[:, n - OUT - 2], wl_o[:, n - OUT - 2]) if n >= OUT + 2 else (wh[:, n % 2], wl[:, n % 2])

        def unit_width(w):
            return DT[XU[w][2]][1] * D if XU[w][0] == "down" else 4 * QF

        block = ctx.enter_context(nc.Block())

        @block.sync
        def _(sp):
            for t in range(NT):
                sp.dma_start(xv[:, t, :], xsrc(x_prompt, x_sample, t)).then_inc(s_x[t], 16)

            def src_of(stage, kind, u):
                if kind[:2] == "br":
                    src, c0 = {"d": w_branch_diff, "n": w_branch_na}[kind[3]], 512 * int(kind[4])
                elif stage == "o":
                    src, c0 = w_out, 512 * int(kind[3])
                elif stage == "g":
                    src, c0 = w_in, 6 * HW + {"d": 0, "n": D}[kind[5]] + 512 * int(kind[6])
                else:
                    src, c0 = w_in, HW * ({"pd": 0, "pn": 3}[stage] + "qkv".index(kind))
                return src[u * 512:(u + 1) * 512, c0:c0 + 512].rearrange("(k p) c -> p k c", p=P)

            for stage, kind, u0, nu in CHUNKS:
                for u in range(u0, u0 + nu):
                    if u >= 2:
                        sp.wait_ge(w_split, u - 1)
                    sp.dma_start(wraw[:, u % 2], src_of(stage, kind, u - u0)).then_inc(w_loaded[u % 2], 16)
                if kind == "out0":
                    sp.wait_ge(S("g", "yn_t"), NT)
                    for t in range(NT):
                        sp.dma_start(xv[:, t, :], xsrc(x_prompt, x_sample, t)).then_inc(s_x[t], 16)
            gate_src = w_expert_gate.rearrange("e (k p) f -> e p k f", p=P)
            up_src = w_expert_up.rearrange("e (k p) f -> e p k f", p=P)
            down_src = w_expert_down.rearrange("e (f p) d -> e p f d", p=P)
            stage_done(sp, 6)
            sp.wait_ge(S("o", "m_t"), 2 * NT)
            with sp.Fori(0, E) as e:
                for w, (kind, q, c) in enumerate(XU):
                    sp.wait_ge(x_split, e * NXU + w + 1)
                    b = w % RAWS
                    if kind == "down":
                        f0, nf = DT[c]
                        src = down_src[e, :, q * FT + f0:q * FT + f0 + nf, :]
                        dst = xraw[:, b, 0:nf * D].rearrange("p (f d) -> p f d", f=nf)
                    else:
                        src = (gate_src if kind == "gate" else up_src)[e, :, 4 * c:4 * c + 4, q * QF:(q + 1) * QF]
                        dst = xraw[:, b, 0:4 * QF].rearrange("p (k f) -> p k f", k=4)
                    sp.dma_start(dst, src).then_inc(x_loaded[b], 16)
            for t in range(NT):
                sp.wait_ge(S("x", "last_added"), 2 * t + 2)
                sp.dma_start(xsrc(y_prompt, y_sample, t), xv[:, t, :]).then_inc(S("x", "stored"), 16)
            sp.wait_ge(S("x", "stored"), 16 * NT)

        @block.gpsimd
        def _(pool):
            nc.gpsimd.memset(napad, 0.0).then_inc(s_nz, 1)
            pool.wait_ge(s_nz, 1)
            pool.dma_start(napad[:, 48:79], na_rpb.rearrange("h r c -> (h r) c")).then_inc(s_nt, 16)
            pool.wait_ge(s_cst, 32)

            def rsqrt(out, in_, w, wait, val, done):
                pool.wait_ge(wait, val)
                nc.gpsimd.tensor_tensor(out, in_, mhalf[:, 0:w], ALU.pow).then_inc(done, 1)

            for t in range(NT):
                rsqrt(nrs[:, t:t + 1], nss[:, t:t + 1], 1, S("n1", "ss"), t + 1, S("n1", "rs"))
            pool.wait_ge(s_nt, 16)
            pool.dma_start(na_dram, napad).then_inc(s_scr, 16)
            pool.wait_ge(s_tc, 1)
            pool.dma_start(t5_dram, t5b).then_inc(s_scr, 16)
            pool.wait_ge(s_scr, 32)
            t5_src = bass.AP(t5_dram.tensor, 0, [[1024, 4], [0, P], [1, 1024]])
            na_src = bass.AP(na_dram.tensor, 0, [[NA_ROWS * 128, 8], [0, 64], [1, NA_ROWS * 128]])
            pool.dma_start(t5_rep, t5_src).then_inc(s_rep, 16)
            pool.dma_start(na_rep, na_src).then_inc(s_rep, 16)
            for i, lv in enumerate((lambda_q1, lambda_k1, lambda_q2, lambda_k2)):
                pool.dma_start(lamv[:, i, :], lv.to_broadcast((P, 64))).then_inc(s_lamv, 16)
            for col, g, w in ((0, diff_q_norm, 64), (1, diff_k_norm, 64), (2, diff_subln_g, 128),
                              (3, na_q_norm, 64), (4, na_k_norm, 64)):
                for r in range(P // w):
                    pool.dma_start(gains[r * w:(r + 1) * w, col:col + 1],
                                   g.rearrange("a d -> d a")).then_inc(s_lamv, 16)
            pool.dma_start(wrt_v, w_router.rearrange("(k p) e -> p k e", p=P)).then_inc(S("rt", "wrt"), 16)

            def load_bias(nh):
                b = nh % 2
                if nh == 0:
                    pool.wait_ge(s_rep, 32)
                if nh >= 2:
                    br, used = ("diff", nh - 1) if nh - 2 < 4 else ("na", nh - 5)
                    pool.wait_ge(S(br, "biased"), HPI * used)
                if nh < 4:
                    src = bass.AP(t5_rep.tensor, nh * P * 1024 + 127, [[1023, 128], [1, BW]])
                    pool.dma_start(bias[:, b, :], src).then_inc(s_b[b], 16)
                else:
                    h = nh - 4
                    for rr in range(2):
                        src = bass.AP(na_rep.tensor, (h * 64 * NA_ROWS + 1 - rr) * 128 + 63,
                                      [[NA_ROWS * 128 - 1, 64], [128, 14], [1, 64]])
                        pool.dma_start(bias[64 * rr:64 * rr + 64, b, :].rearrange("p (j k) -> p j k", j=14),
                                       src).then_inc(s_b[b], 16)

            def mask_bias(nh):
                b = nh % 2
                pool.wait_ge(s_b[b], 32 * (nh // 2 - 2) + 64)
                v = bias[:, b, :].rearrange("p (j k) -> p j k", j=14)
                nc.gpsimd.tensor_tensor(v, v, mask.unsqueeze(1).to_broadcast((P, 14, 64)), ALU.add).then_inc(s_bm, 1)

            def norm_rs(stage, jobs, w):
                for j in range(jobs):
                    rsqrt(rs[:, j % 4, 0:w], ss[:, j % 4, 0:w], w, S(stage, "ss"), j + 1, S(stage, "rs"))

            norm_rs("pd", 12, 8)
            load_bias(0)
            load_bias(1)
            load_bias(2)
            load_bias(3)
            load_bias(4)
            load_bias(5)
            norm_rs("yd", NT, 4)
            mask_bias(4)
            mask_bias(5)
            norm_rs("pn", 12, 8)
            for nh in range(6, 12):
                load_bias(nh)
                mask_bias(nh)
            pool.wait_ge(S("o", "m_t"), 2 * NT)
            pool.dma_start(g2b, norm2_g.to_broadcast((P, D))).then_inc(S("rt", "g2"), 16)
            for t in range(NT):
                rsqrt(nrs[:, t:t + 1], nss[:, t:t + 1], 1, S("n2", "ss"), t + 1, S("n2", "rs"))
                pool.wait_ge(S("n2", "hn"), t + 1)
                pool.dma_start(t_dram[t * P:(t + 1) * P, :], tn[:, t % 2, :]).then_inc(S("n2", f"stored{t % 2}"), 16)
            nc.gpsimd.iota(iota_tok, pattern=[[1, N]], base=0, channel_multiplier=0,
                           allow_small_or_imprecise_dtypes=True).then_inc(S("x", "iota"), 1)
            pool.wait_ge(S("n2", "stored0"), 48)
            pool.wait_ge(S("n2", "stored1"), 48)
            pool.wait_ge(S("rt", "tables"), 1)
            for e in range(E + 1):
                if e == 1:
                    pool.wait_ge(S("x", "misc"), PRE)
                elif e > 1:
                    pool.wait_ge(S("x", "misc"), PRE + NU * (e - 2) + use_no("tokens", 1) + 1)
                col = min(e, E - 1) + 1
                pool.indirect_dma_start(xe, None, t_dram, bass.IndirectOffsetOnAxis(ap=idxi[:, col:col + 1], axis=0)
                                        ).then_inc(S("x", "xe"), 16)
            pool.wait_ge(S("x", "xe"), 16 * (E + 1))

        @block.tensor
        def _(pe):
            mm = nc.tensor.matmul
            pe.sem_inc(x_used, SPLITS)
            pe.wait_ge(s_cst, 32)
            pe.wait_ge(s_tab, 32)
            for b in range(2):
                i = mm(PS[0:4, 2 + b, :], t5t, t5h[:, b * 512:(b + 1) * 512], start=True, stop=True)
            i.then_inc(s_tm, 1)

            def split_product(out, sh, sl, mh, ml, first, last):
                mm(out, sh, mh, start=first, stop=False)
                mm(out, sh, ml, start=False, stop=False)
                return mm(out, sl, mh, start=False, stop=last)

            for t in range(NT):
                pe.wait_ge(S("n1", "hn"), t + 1)
                for q in range(2):
                    j = 2 * t + q
                    if j >= 4:
                        pe.wait_ge(S("n1", "tev"), j - 3)
                    for k in range(4):
                        i = nc.tensor.transpose(PS[:, 4 + j % 4, k * P:(k + 1) * P],
                                                hn[:, t % 2, (4 * q + k) * P:(4 * q + k + 1) * P], ident)
                    i.then_inc(S("n1", "tr"), 1)

            def transposes(stage, jt, src, done):
                if jt >= 2:
                    pe.wait_ge(S(stage, "tev"), jt - 1)
                for c in range(4):
                    i = nc.tensor.transpose(PS[:, 6 + jt % 2, c * P:(c + 1) * P], src[:, c * P:(c + 1) * P], ident)
                i.then_inc(S(stage, done), 1)

            def chunk_steps(chunks):
                return [(c, u, t) for c in range(len(chunks)) for u in range(chunks[c][3]) for t in range(NT)]

            def chunk_product(chunks, c, u, t, sh, sl, bank_free):
                stage, kind, u0, nu = chunks[c]
                n = u0 + u
                if t == 0:
                    pe.wait_ge(w_split, n + 1)
                if u == 0:
                    bank_free(c, t)
                for k in range(4):
                    i = split_product(PS[:, t, :], sh[:, 4 * u + k, t * P:(t + 1) * P],
                                      sl[:, 4 * u + k, t * P:(t + 1) * P], wh[:, n % 2, k], wl[:, n % 2, k],
                                      u == 0 and k == 0, u == nu - 1 and k == 3)
                i.then_inc(w_prod, 1)

            def after_attention(br, t):
                pe.wait_ge(S(br, "biased" if t < 4 else "aT"), len(ATT[br]))

            def project(stage, before):
                chunks = [c for c in CHUNKS if c[0] == stage]
                steps = chunk_steps(chunks)
                def bank_free(c, t):
                    if c > 0:
                        pe.wait_ge(S(stage, "pused"), NT * (c - 1) + t + 1)
                    elif before is not None:
                        after_attention(before, t)
                    else:
                        if t == 2:
                            pe.wait_ge(s_tc, 1)
                        pe.wait_ge(S("n1", "tev"), 2 * (t + 1) if t < 4 else 2 * NT)

                done_at, jt = [], 0
                for n, (c, u, t) in enumerate(steps):
                    if before is None or n >= START_EARLY:
                        chunk_product(chunks, c, u, t, hTh, hTl, bank_free)
                    if u == 1 and c < 2:
                        done_at.append(n)
                    while jt < len(done_at) and n >= done_at[jt] + 2:
                        if jt == 0 and before is not None:
                            pe.wait_ge(S(before, "out"), len(ATT[before]))
                        pe.wait_ge(S(stage, "qn"), jt + 1)
                        transposes(stage, jt, qn[:, jt % 2, :], "tr")
                        jt += 1

            def attend(br, stage, following):
                pe.wait_ge(S(stage, "tev"), 2 * NT)
                pe.wait_ge(S(stage, "pused"), 2 * NT + 4)
                chunks = [c for c in CHUNKS if c[0] == following]
                L = ATT[br]
                nm = 2 if br == "diff" else 1
                for step in range(len(L) + 5):
                    if step < len(L):
                        h, qt, t0, nt = L[step]
                        ring = 4 // nm
                        if step >= ring:
                            pe.wait_ge(S(br, "biased"), step - ring + 1)
                        for m in range(nm):
                            c, r = (h, m) if br == "diff" else (h // 2, h % 2)
                            i = mm(PS[:, nm * (step % ring) + m, 0:nt * P],
                                   qT[:, c, (t0 + qt) * P:(t0 + qt + 1) * P],
                                   kT[r][:, c, t0 * P:(t0 + nt) * P], start=True, stop=True)
                        i.then_inc(S(br, "log"), 1)
                    a = step - 5
                    if 0 <= a < len(L):
                        h, qt, t0, nt = L[a]
                        pe.wait_ge(S(br, "aT"), a + 1)
                        if a >= 2:
                            pe.wait_ge(S(br, "out"), a - 1)
                        w = P if br == "diff" else 64
                        for c in range(nt):
                            i = mm(PS[:, 6 + a % 2, 0:w], aT[:, a % 2, c * P:(c + 1) * P],
                                   vv[:, t0 + c, h * w:(h + 1) * w], start=c == 0, stop=c == nt - 1)
                        i.then_inc(S(br, "pv"), 1)
                    a = step - 3
                    if 0 <= a < len(L):
                        h, qt, t0, nt = L[a]
                        if a == 0:
                            pe.wait_ge(S(stage, "pused"), 3 * NT)
                        pe.wait_ge(S(br, "probs"), a + 1)
                        if a >= 2:
                            pe.wait_ge(S(br, "aT"), a - 1)
                        for c in range(nt):
                            i = nc.tensor.transpose(PS[:, 4 + a % 2, c * P:(c + 1) * P],
                                                    sT[:, a % 4, 0, c * P:(c + 1) * P], ident)
                        i.then_inc(S(br, "tr"), 1)
                    if step >= len(L):
                        chunk_product(chunks, 0, 0, step - len(L), hTh, hTl, lambda c, t: after_attention(br, t))

            project("pd", None)
            pe.wait_ge(s_kz, 2)
            attend("diff", "pd", "pn")
            project("pn", "diff")
            attend("na", "pn", "g")
            chunks = [c for c in CHUNKS if c[0] == "g"]

            def g_bank_free(c, t):
                if c > 0:
                    kind = chunks[c - 1][1]
                    pe.wait_ge(S("g", "sig" if kind[:4] == "gate" else "mul"), NT * ((c - 1) // 2) + t + 1)
                else:
                    after_attention("na", t)

            def transpose_merged(j):
                t, q = j % NT, j // NT
                if j == 0:
                    pe.wait_ge(S("g", "tev"), 2 * NT)
                    pe.wait_ge(S("g", "mul"), 3 * NT)
                elif j >= NT:
                    pe.wait_ge(S("g", "mul"), 3 * NT + t + 1)
                if j >= 2:
                    pe.wait_ge(S("o", "tev"), j - 1)
                for k in range(4):
                    i = nc.tensor.transpose(PS[:, 6 + j % 2, k * P:(k + 1) * P],
                                            mm_[:, t, (4 * q + k) * P:(4 * q + k + 1) * P], ident)
                i.then_inc(S("o", "m_t"), 1)

            for n, (c, u, t) in enumerate(chunk_steps(chunks)):
                kind = chunks[c][1]
                if kind == "gate_d0" and u == 1:
                    if t == 0:
                        pe.wait_ge(S("na", "out"), len(ATT["na"]))
                        pe.wait_ge(S("yd", "qn"), NT)
                    transposes("g", t, y_tok["diff"][:, t, :], "yd_t")
                if kind == "gate_n0" and u == 1:
                    transposes("g", NT + t, y_tok["na"][:, t, :], "yn_t")
                if kind == "gate_n1" and u == 1:
                    transpose_merged(t)
                if kind[:2] == "br" and u == 0 and t == 0:
                    pe.wait_ge(S("g", "tev"), NT if kind[3] == "d" else 2 * NT)
                sh, sl = (yTh, yTl) if kind[:2] == "br" else (hTh, hTl)
                if n >= START_EARLY:
                    chunk_product(chunks, c, u, t, sh, sl, g_bank_free)
                if kind == "br_n1" and t > 0:
                    transpose_merged(NT + t - 1)
            transpose_merged(2 * NT - 1)
            pe.wait_ge(S("g", "mul"), 3 * NT + 4)
            def out_product(t, c):
                if t >= 2:
                    pe.wait_ge(S("o", "added"), 2 * (t - 2) + c + 1)
                for u in range(2):
                    n = OUT + 2 * c + u
                    if t == 0:
                        pe.wait_ge(w_split, n + 1)
                    if c == 0:
                        pe.wait_ge(S("o", "tev"), u * NT + t + 1)
                    uh, ul = split_slot(n)
                    for k in range(4):
                        i = split_product(PS[:, 2 * (t % 2) + c, :], hTh[:, 4 * u + k, t * P:(t + 1) * P],
                                          hTl[:, 4 * u + k, t * P:(t + 1) * P], uh[:, k], ul[:, k],
                                          u == 0 and k == 0, u == 1 and k == 3)
                    i.then_inc(w_prod, 1)

            def transpose_normed(t):
                pe.wait_ge(S("n2", "hn"), t + 1)
                for q in range(2):
                    j = 2 * t + q
                    if j >= 2:
                        pe.wait_ge(S("n2", "tev"), j - 1)
                    for k in range(4):
                        i = nc.tensor.transpose(PS[:, 4 + q, k * P:(k + 1) * P],
                                                tn[:, t % 2, (4 * q + k) * P:(4 * q + k + 1) * P], ident)
                    i.then_inc(S("n2", "tr"), 1)

            def router_logits(t):
                pe.wait_ge(S("n2", "tev"), 2 * t + 2)
                for k in range(KD):
                    i = mm(PS[:, 6, t * E:(t + 1) * E], tT[:, t % 2, k, :], wrt_v[:, k, :],
                           start=k == 0, stop=k == KD - 1)
                i.then_inc(S("rt", "logits"), 1)

            pe.wait_ge(S("rt", "wrt"), 16)
            for t in range(NT + 2):
                for i, (tile, c) in enumerate(OUT_ORDER[2 * t:2 * t + 2]):
                    if i == 1 and t >= 2:
                        router_logits(t - 2)
                    out_product(tile, c)
                if t >= NT:
                    router_logits(t - 2)
                if 1 <= t <= NT:
                    transpose_normed(t - 1)
            pe.wait_ge(S("rt", "aff"), 1)
            for t in range(NT):
                i = nc.tensor.transpose(PS[0:E, t // 4, (t % 4) * P:(t % 4 + 1) * P], aff[:, t, :], ident)
            i.then_inc(S("rt", "affT"), 1)
            pe.wait_ge(S("rt", "rank"), 1)
            for t in range(NT):
                i = nc.tensor.transpose(PS[:, 7, t * E:(t + 1) * E], cumT[:, t * P:(t + 1) * P], ident[0:E, 0:E])
            i.then_inc(S("rt", "rkT"), 1)
            for t in range(NT):
                if t == 0:
                    pe.wait_ge(S("rt", "parts"), 1)
                pe.wait_ge(S("rt", "G"), t + 1)
                smp = t >= 2
                w, p0 = (CS, 0) if smp else (CP, CS)
                first = 2 if smp else 0
                last = NT - 1 if smp else 1
                for e in range(E):
                    i = mm(PS[p0:p0 + w, 3 if smp else 2, 6 * e:6 * e + 6], G[:, t % 4, e, 0:w],
                           R3[:, t, e].rearrange("p m c -> p (m c)"),
                           start=(t == first and e == 0), stop=t == last, skip_group_check=True)
                i.then_inc(S("rt", "slots"), 1)

            def transpose_tokens(q):
                for k in range(4):
                    i = nc.tensor.transpose(PS[:, 6 + q % 2, k * CAP:(k + 1) * CAP],
                                            xe[:, (4 * q + k) * P:(4 * q + k + 1) * P], ident[0:CAP, 0:CAP])
                i.then_inc(S("x", "misc"), 1)

            def scatter(j, bank):
                t, half = divmod(j, 2)
                lhs = scat[:, t * P:(t + 1) * P]
                cols = slice(half * 512, (half + 1) * 512)
                mm(PS[:, bank, :], lhs, yeh[:, cols], start=True, stop=False)
                mm(PS[:, bank, :], lhs, yel[:, cols], start=False, stop=True).then_inc(S("x", "misc"), 1)

            stage_done(pe, 7)
            pe.wait_ge(S("x", "xe"), 16)
            for q in range(PRE):
                transpose_tokens(q)
            pe.wait_ge(S("x", "misc_read"), PRE)
            xT = [a.rearrange("p (k s) -> p k s", k=KD) for a in (xTh, xTl)]
            hT = [a.rearrange("p (f s) -> p f s", f=FT) for a in (hidh, hidl)]
            with pe.Fori(0, E) as e:
                for w, (kind, q, c) in enumerate(XU):
                    b = w % SPLITS
                    pe.wait_ge(x_split, e * NXU + w + 1 + RAWS)
                    if kind == "down":
                        f0, nf = DT[c]
                        uh, ul = (a[:, b, 0:nf * D].rearrange("p (f d) -> p f d", f=nf) for a in (xh, xl))
                        last_round = [r for r, (r0, rn) in enumerate(HR) if r0 < f0 + nf][-1]
                        pe.wait_ge(S("x", "misc_read"), e * NU + PRE + use_no("hidden", 3 * q + last_round) + 1)
                        for f in range(nf):
                            g = f0 + f
                            for half in range(2):
                                cols = slice(half * 512, (half + 1) * 512)
                                i = split_product(PS[0:CAP, 4 + half, :], hT[0][:, g, :], hT[1][:, g, :],
                                                  uh[:, f, cols], ul[:, f, cols], q == 0 and g == 0,
                                                  q == 1 and g == FT - 1)
                    else:
                        uh, ul = (a[:, b, 0:4 * QF].rearrange("p (k f) -> p k f", k=4) for a in (xh, xl))
                        if kind == "gate" and c == 0 and q > 0:
                            pe.wait_ge(S("x", "silu"), e * 4 + q)
                        b0 = 0 if kind == "gate" else 2
                        for k in range(4):
                            for half in range(2):
                                cols = slice(half * QC, (half + 1) * QC)
                                i = split_product(PS[0:CAP, b0 + half, 0:QC], xT[0][:, 4 * c + k, :],
                                                  xT[1][:, 4 * c + k, :], uh[:, k, cols], ul[:, k, cols],
                                                  c == 0 and k == 0, c == 1 and k == 3)
                    i.then_inc(x_used, 1)
                    for what, j in MISC.get(w, []):
                        u = use_no(what, j)
                        pe.wait_ge(S("x", "misc_read"), e * NU + PRE + u - 1)
                        if what == "tokens":
                            if j == 0:
                                pe.wait_ge(S("x", "xe"), e * 16 + 32)
                            transpose_tokens(j)
                        elif what == "hidden":
                            h, r = divmod(j, 3)
                            f0, nf = HR[r]
                            need = 2 * h + (1 if (f0 + nf) * P <= QF else 2)
                            pe.wait_ge(S("x", "hidden"), e * 4 + need)
                            for f in range(nf):
                                i = nc.tensor.transpose(PS[:, 6 + u % 2, f * CAP:(f + 1) * CAP],
                                                        hid[:, (f0 + f) * P:(f0 + f + 1) * P], ident[0:CAP, 0:CAP])
                            i.then_inc(S("x", "misc"), 1)
                        else:
                            if j == 0:
                                pe.wait_ge(S("x", "ye_low"), e + 1)
                                pe.wait_ge(S("x", "onehot"), e + 1)
                            scatter(j, 6 + u % 2)
            pe.wait_ge(S("x", "onehot"), E + 1)
            pe.wait_ge(S("x", "ye_low"), E + 1)
            for j in range(12):
                pe.wait_ge(S("x", "misc_read"), E * NU + PRE + j - 1)
                scatter(j, 6 + j % 2)

        @block.scalar
        def _(act):
            a_ = nc.scalar.activation
            unit = [0]

            def split_units(upto):
                while unit[0] < min(upto, UNITS):
                    n = unit[0]
                    act.wait_ge(w_loaded[n % 2], 16 * (n // 2 + 1))
                    if n >= OUT + 2:
                        act.wait_ge(s_phd, 6)
                    elif n >= 2:
                        act.wait_ge(w_prod, NT * (n - 1))
                    a_(split_slot(n)[0], wraw[:, n % 2], ACT.Copy).then_inc(w_high, 1)
                    unit[0] += 1

            for dst, src, done in ((cst, consts, s_cst), (g1b, norm1_g.to_broadcast((P, D)), s_cst),
                                   (t5h, t5_onehot, s_tab), (t5t, rel_bias, s_tab)):
                act.dma_start(dst, src).then_inc(done, 16)
            for t in range(NT):
                act.wait_ge(s_x[t], 16)
                if t > 0:
                    act.wait_ge(S("n1", "sq"), t)
                a_(junk, xv[:, t, :], ACT.Square, accum_out=nss[:, t:t + 1]).then_inc(S("n1", "sq"), 1)
            act.wait_ge(s_tm, 1)
            a_(t5b, PS[0:4, 2:4, :].rearrange("p b n -> p (b n)"), ACT.Copy).then_inc(s_tc, 1)
            for t in range(NT):
                for q in range(2):
                    j = 2 * t + q
                    act.wait_ge(S("n1", "tr"), j + 1)
                    a_(hTh[:, 4 * q:4 * q + 4, t * P:(t + 1) * P],
                       PS[:, 4 + j % 4, :].rearrange("p (k n) -> p k n", k=4), ACT.Copy).then_inc(S("n1", "high"), 1)
                if t in (1, 3):
                    split_units(t // 2 + 1)
            act.wait_ge(S("n1", "high"), 2 * NT)
            act.sem_inc(s_pha, 1)
            act.wait_ge(s_lam, 1)
            a_(lam[:, 2:4], lam[:, 0:2], ACT.Exp).then_inc(s_lae, 1)

            def square(stage, j, src):
                if j >= 2:
                    act.wait_ge(S(stage, "ss"), j - 1)
                a_(sq[:, j % 2, :], src, ACT.Square).then_inc(S(stage, "sq"), 1)

            def evac_t(stage, jt, g0):
                c, t = divmod(jt, NT)
                act.wait_ge(S(stage, "tr"), jt + 1)
                src = PS[:, 6 + jt % 2, :].rearrange("p (c n) -> p c n", c=4)
                gain = gains[:, g0 + c:g0 + c + 1]
                if c == 0:
                    i = a_(qT[:, :, t * P:(t + 1) * P], src, ACT.Copy, scale=gain)
                else:
                    for r in range(2):
                        rows = slice(64 * r, 64 * r + 64)
                        i = a_(kT[r][rows, :, t * P:(t + 1) * P], src[rows], ACT.Copy, scale=gain[rows])
                i.then_inc(S(stage, "tev"), 1)

            def project(stage, g0):
                chunks = [c for c in CHUNKS if c[0] == stage]
                jt = 0
                for c, (_, kind, u0, nu) in enumerate(chunks):
                    split_units(u0 + nu + 1)
                    for t in range(NT):
                        j = NT * c + t
                        if c < 2:
                            product_done(act, chunks[c], t)
                            square(stage, j, PS[:, t, :])
                        if jt <= j - 2 and jt < 2 * NT:
                            evac_t(stage, jt, g0)
                            jt += 1
                    while c == 1 and jt < 2 * NT:
                        evac_t(stage, jt, g0)
                        jt += 1
                    split_units(u0 + nu + 2)
                act.wait_ge(S(stage, "tev"), 2 * NT)
                act.sem_inc(s_pha, 1)

            def attend(br):
                L = ATT[br]
                nm = 2 if br == "diff" else 1
                for step in range(len(L) + 3):
                    a = step
                    if a < len(L):
                        n = L[a][3] * P
                        act.wait_ge(S(br, "biased"), a + 1)
                        for m in range(nm):
                            v = sT[:, a % 4, m, 0:n]
                            i = a_(v, v, ACT.Exp, bias=mx[:, a % 4, m:m + 1], scale=-1.0,
                                   accum_out=sm[:, a % 4, m:m + 1])
                        i.then_inc(S(br, "exp"), 1)
                    a = step - 1
                    if br == "diff" and 0 <= a < len(L):
                        n = L[a][3] * P
                        act.wait_ge(S(br, "ratio"), a + 1)
                        v = sT[:, a % 4, 1, 0:n]
                        a_(v, v, ACT.Copy, scale=ri[:, a % 8, 1:2]).then_inc(S(br, "second"), 1)
                    a = step - 3
                    if a >= 0:
                        n = L[a][3] * P
                        act.wait_ge(S(br, "tr"), a + 1)
                        if a >= 2:
                            act.wait_ge(S(br, "pv"), a - 1)
                        a_(aT[:, a % 2, 0:n], PS[:, 4 + a % 2, 0:n], ACT.Copy).then_inc(S(br, "aT"), 1)
                act.wait_ge(S(br, "aT"), len(L))
                act.sem_inc(s_pha, 1)

            project("pd", 0)
            attend("diff")
            act.wait_ge(S("diff", "out"), len(ATT["diff"]))
            for t in range(NT):
                square("yd", t, y_tok["diff"][:, t, :])
            act.wait_ge(S("yd", "ss"), NT)
            project("pn", 3)
            attend("na")

            def high_t(stage, jt, dst, signal, val, gain=None):
                act.wait_ge(signal, val)
                src = PS[:, 6 + jt % 2, :].rearrange("p (c n) -> p c n", c=4)
                i = a_(dst, src, ACT.Copy) if gain is None else a_(dst, src, ACT.Copy, scale=gain)
                i.then_inc(S(stage, "high"), 1)

            def merged_high(j):
                t, q = j % NT, j // NT
                high_t("o", j, hTh[:, 4 * q:4 * q + 4, t * P:(t + 1) * P], S("o", "m_t"), j + 1)

            chunks = [c for c in CHUNKS if c[0] == "g"]
            for c, (_, kind, u0, nu) in enumerate(chunks):
                split_units(u0 + nu + 1)
                if kind[:4] == "gate":
                    half = int(kind[6])
                    for t in range(NT):
                        cols = slice(t * P, (t + 1) * P)
                        if kind == "gate_d0":
                            high_t("g", t, yTh[:, :, cols], S("g", "yd_t"), t + 1, gains[:, 2:3])
                        elif kind == "gate_n0":
                            high_t("g", NT + t, yTh[:, :, cols], S("g", "yn_t"), t + 1)
                        elif kind == "gate_n1":
                            merged_high(t)
                        product_done(act, chunks[c], t)
                        if kind == "gate_n1":
                            act.wait_ge(S("g", "mul"), 2 * NT + t + 1)
                        dst = mm_[:, t, half * 512:(half + 1) * 512] if kind[5] == "d" else sg_n[:, t, :]
                        a_(dst, PS[:, t, :], ACT.Sigmoid).then_inc(S("g", "sig"), 1)
                if kind == "br_n1":
                    for j in range(NT, NT + 4):
                        merged_high(j)
                split_units(u0 + nu + 2)
            act.wait_ge(S("g", "sig"), 4 * NT)
            act.sem_inc(s_pha, 1)
            for j in range(NT + 4, 2 * NT):
                merged_high(j)
            split_units(UNITS)
            act.wait_ge(w_split, UNITS)
            for t in range(NT + 1):
                if t < NT:
                    act.wait_ge(S("o", "added"), 2 * t + 2)
                    if t >= 2:
                        act.wait_ge(S("n2", "tr"), 2 * (t - 1))
                        act.wait_ge(S("n2", f"stored{t % 2}"), 16 * (t // 2))
                    a_(tn[:, t % 2, :], xv[:, t, :], ACT.Square, accum_out=nss[:, t:t + 1]).then_inc(S("n2", "sq"), 1)
                if t > 0:
                    for q in range(2):
                        j = 2 * (t - 1) + q
                        act.wait_ge(S("n2", "tr"), j + 1)
                        if t >= 3:
                            act.wait_ge(S("rt", "logits"), t - 2)
                        a_(tT[:, (t - 1) % 2, 4 * q:4 * q + 4, :], PS[:, 4 + q, :].rearrange("p (k n) -> p k n", k=4),
                           ACT.Copy).then_inc(S("n2", "tev"), 1)

            def unit_high(e, w):
                act.wait_ge(x_loaded[w % RAWS], e * 16 * (NXU // RAWS) + 16 * (w // RAWS + 1))
                act.wait_ge(x_used, e * NXU + w + 1)
                n = unit_width(w)
                a_(xh[:, w % SPLITS, 0:n], xraw[:, w % RAWS, 0:n], ACT.Copy).then_inc(x_high, 1)

            unit_high(0, 0)
            act.wait_ge(S("rt", "shift"), 1)
            for t in range(NT):
                i = a_(aff[:, t, :], aff[:, t, :], ACT.Exp, bias=rmx[:, t:t + 1], accum_out=rsm[:, t:t + 1])
            i.then_inc(S("rt", "exp"), 1)
            for b in range(2):
                act.wait_ge(S("n2", f"stored{b}"), 48)
            for w in range(1, SPLITS):
                unit_high(0, w)
            act.wait_ge(S("rt", "exp"), 1)
            act.sem_inc(s_pha, 1)

            def misc_high(what, j, n, bank):
                act.wait_ge(S("x", "misc"), n)
                c0, w = (j * 4 * CAP, 4 * CAP) if what == "tokens" else (HR[j % 3][0] * CAP, HR[j % 3][1] * CAP)
                dst = xTh if what == "tokens" else hidh
                a_(dst[:, c0:c0 + w], PS[:, bank, 0:w], ACT.Copy).then_inc(S("x", "misc_high"), 1)

            for q in range(PRE):
                misc_high("tokens", q, q + 1, 6 + q)

            def expert_body(e, last):
                for u in range(NXU):
                    if u == 0:
                        act.wait_ge(S("x", "cur"), e + 1)
                        for half in range(2):
                            i = a_(yeh[:, half * 512:(half + 1) * 512], PS[0:CAP, 4 + half, :], ACT.Copy,
                                   scale=cur_g)
                        i.then_inc(S("x", "ye_high"), 1)
                    kind, q, c = XU[u]
                    if kind == "gate" and c == 1:
                        act.wait_ge(x_used, e * NXU + u + 1 + SPLITS)
                        if q > 0:
                            act.wait_ge(S("x", "hidden"), e * 4 + q)
                        a_(sg.rearrange("p (h f) -> p h f", h=2), PS[0:CAP, 0:2, 0:QC], ACT.Silu
                           ).then_inc(S("x", "silu"), 1)
                    for what, j in MISC.get(u, []):
                        if what != "scatter":
                            n = use_no(what, j)
                            misc_high(what, j, e * NU + PRE + n + 1, 6 + n % 2)
                    w = u + SPLITS
                    if w < NXU:
                        unit_high(e, w)
                    elif not last:
                        unit_high(e + 1, w - NXU)

            with act.Fori(0, E - 1) as e:
                expert_body(e, False)
            expert_body(E - 1, True)
            act.wait_ge(S("x", "cur"), E + 1)
            act.wait_ge(x_used, NXU * E + SPLITS)
            for half in range(2):
                i = a_(yeh[:, half * 512:(half + 1) * 512], PS[0:CAP, 4 + half, :], ACT.Copy, scale=cur_g)
            i.then_inc(S("x", "ye_high"), 1)

        @block.vector
        def _(dve):
            v = nc.vector

            def link(ins):
                chain_count[0] += 1
                ins.then_inc(s_dv, 1)
                dve.wait_ge(s_dv, chain_count[0])

            unit = [0]

            def low(out, src, high):
                return v.tensor_tensor(out, src, high.bitcast(F32), ALU.subtract)

            def split_units(upto):
                while unit[0] < min(upto, UNITS):
                    n = unit[0]
                    dve.wait_ge(w_high, n + 1)
                    high, lows = split_slot(n)
                    low(lows, wraw[:, n % 2], high).then_inc(w_split, 1)
                    unit[0] += 1

            dve.sem_inc(x_split, RAWS - 1)
            dve.wait_ge(s_cst, 32)

            def mean_eps(out, in_, w, done):
                return v.tensor_scalar(out, in_, 1.0 / w, EPS, ALU.mult, ALU.add).then_inc(done, 1)

            def norm_tokens(stage, gb, dst, bufs_free, then):
                for t in range(NT + 2):
                    if t < NT:
                        dve.wait_ge(S(stage, "sq"), t + 1)
                        mean_eps(nss[:, t:t + 1], nss[:, t:t + 1], D, S(stage, "ss"))
                    if 0 < t <= NT:
                        u = t - 1
                        dve.wait_ge(S(stage, "rs"), u + 1)
                        bufs_free(u)
                        v.scalar_tensor_tensor(dst[:, u % 2, :], xv[:, u, :], nrs[:, u:u + 1], gb, ALU.mult,
                                               ALU.mult).then_inc(S(stage, "hn"), 1)
                    if t > 1:
                        then(t - 2)

            def hn_free(u):
                if u >= 2:
                    dve.wait_ge(S("n1", "tr"), 2 * (u - 1))

            def hT_low(t):
                for q in range(2):
                    j = 2 * t + q
                    dve.wait_ge(S("n1", "high"), j + 1)
                    dst = (slice(None), slice(4 * q, 4 * q + 4), slice(t * P, (t + 1) * P))
                    low(hTl[dst], PS[:, 4 + j % 4, :].rearrange("p (k n) -> p k n", k=4), hTh[dst]
                        ).then_inc(S("n1", "tev"), 1)
                if t in (1, 3):
                    split_units(t // 2 + 1)

            norm_tokens("n1", g1b, hn, hn_free, hT_low)
            dve.wait_ge(S("n1", "tev"), 2 * NT)
            dve.sem_inc(s_phd, 1)
            for r in range(2):
                v.memset(kT[r][64 * (1 - r):64 * (2 - r)], 0.0).then_inc(s_kz, 1)
            dve.wait_ge(s_lamv, 16 * 13)
            for m in range(2):
                i = v.tensor_tensor(lamv[:, 2 * m, :], lamv[:, 2 * m, :], lamv[:, 2 * m + 1, :], ALU.mult)
            link(i)
            for m in range(2):
                i = v.tensor_reduce(lam[:, m:m + 1], lamv[:, 2 * m, :], AX.X, ALU.add)
            i.then_inc(s_lam, 1)
            dve.wait_ge(s_lam, 1)
            for c, s_ in ((0, 0.125), (2, 1.0 - LAM0), (3, 0.125)):
                i = v.tensor_scalar(gains[:, c:c + 1], gains[:, c:c + 1], s_, None, ALU.mult)
            dve.wait_ge(s_lae, 1)
            link(v.scalar_tensor_tensor(lam[:, 0:1], lam[:, 2:3], LAM0, lam[:, 3:4], ALU.add, ALU.subtract))

            def reduce_sq(stage, j, heads, hd):
                dve.wait_ge(S(stage, "sq"), j + 1)
                if j >= 4:
                    dve.wait_ge(S(stage, "qn"), j - 3)
                link(v.tensor_reduce(ss[:, j % 4, 0:heads], sq[:, j % 2, :].rearrange("p (h d) -> p h d", h=heads),
                                     AX.X, ALU.add))
                mean_eps(ss[:, j % 4, 0:heads], ss[:, j % 4, 0:heads], hd, S(stage, "ss"))

            def scale_q(stage, j, dst, src, heads, hd):
                dve.wait_ge(S(stage, "rs"), j + 1)
                r = rs[:, j % 4, 0:heads].unsqueeze(2).to_broadcast((P, heads, hd))
                return v.tensor_tensor(dst.rearrange("p (h d) -> p h d", h=heads),
                                       src.rearrange("p (h d) -> p h d", h=heads), r, ALU.mult
                                       ).then_inc(S(stage, "qn"), 1)

            def scale_proj(stage, j):
                if j >= 2:
                    dve.wait_ge(S(stage, "tr"), j - 1)
                scale_q(stage, j, qn[:, j % 2, :], PS[:, j % NT, :], 8, 64)
                dve.wait_ge(S(stage, "qn"), j + 1)
                dve.sem_inc(S(stage, "pused"), 1)

            def project(stage):
                chunks = [c for c in CHUNKS if c[0] == stage]
                for c, (_, kind, u0, nu) in enumerate(chunks):
                    split_units(u0 + nu + 1)
                    for t in range(NT):
                        j = NT * c + t
                        if c < 2:
                            reduce_sq(stage, j, 8, 64)
                            if t > 0:
                                scale_proj(stage, j - 1)
                        else:
                            product_done(dve, chunks[c], t)
                            v.tensor_copy(vv[:, t, :], PS[:, t, :]).then_inc(S(stage, "pused"), 1)
                    if c < 2:
                        scale_proj(stage, NT * c + NT - 1)
                    split_units(u0 + nu + 2)
                dve.wait_ge(S(stage, "pused"), 3 * NT)
                dve.sem_inc(s_phd, 1)

            def attend(br):
                L = ATT[br]
                nm = 2 if br == "diff" else 1
                for step in range(len(L) + 5):
                    a = step
                    if a < len(L):
                        h, qt, t0, nt = L[a]
                        n = nt * P
                        nh = h if br == "diff" else 4 + h
                        b = nh % 2
                        if a % HPI == 0:
                            if br == "diff":
                                dve.wait_ge(s_b[b], 16 * (h // 2 + 1))
                            else:
                                dve.wait_ge(s_bm, h + 1)
                        dve.wait_ge(S(br, "log"), a + 1)
                        if a >= 4:
                            dve.wait_ge(S(br, "tr"), a - 3)
                        c0 = 384 - 128 * qt
                        for m in range(nm):
                            i = v.tensor_tensor_reduce(
                                out=sT[:, a % 4, m, 0:n], in0=PS[:, nm * (a % (4 // nm)) + m, 0:n], in1=bias[:, b, c0:c0 + n],
                                scale=-1.0, scalar=3.0e38, op0=ALU.add, op1=ALU.min,
                                accum_out=mx[:, a % 4, m:m + 1])
                        i.then_inc(S(br, "biased"), 1)
                    a = step - 1
                    if 0 <= a < len(L):
                        n = L[a][3] * P
                        dve.wait_ge(S(br, "exp"), a + 1)
                        if br == "diff":
                            link(v.reciprocal(ri[:, a % 8, :], sm[:, a % 4, :]))
                            v.tensor_tensor(ri[:, a % 8, 1:2], ri[:, a % 8, 1:2], lam[:, 0:1], ALU.mult
                                            ).then_inc(S(br, "ratio"), 1)
                        else:
                            v.reciprocal(ri[:, a % 8, 0:1], sm[:, a % 4, 0:1]).then_inc(S(br, "probs"), 1)
                    a = step - 2
                    if br == "diff" and 0 <= a < len(L):
                        n = L[a][3] * P
                        dve.wait_ge(S(br, "second"), a + 1)
                        v.scalar_tensor_tensor(sT[:, a % 4, 0, 0:n], sT[:, a % 4, 0, 0:n], ri[:, a % 8, 0:1],
                                               sT[:, a % 4, 1, 0:n], ALU.mult, ALU.subtract
                                               ).then_inc(S(br, "probs"), 1)
                    a = step - 5
                    if 0 <= a < len(L):
                        h, qt, t0, nt = L[a]
                        dve.wait_ge(S(br, "pv"), a + 1)
                        w = P if br == "diff" else 64
                        dst = y_tok[br][:, t0 + qt, h * w:(h + 1) * w]
                        if br == "diff":
                            i = v.tensor_copy(dst, PS[:, 6 + a % 2, 0:w])
                        else:
                            i = v.tensor_scalar(dst, PS[:, 6 + a % 2, 0:w], ri[:, a % 8, 0:1], None, ALU.mult)
                        i.then_inc(S(br, "out"), 1)
                dve.wait_ge(S(br, "out"), len(L))
                dve.sem_inc(s_phd, 1)

            project("pd")
            attend("diff")
            for t in range(NT + 1):
                if t < NT:
                    reduce_sq("yd", t, 4, 128)
                if t > 0:
                    y = y_tok["diff"][:, t - 1, :]
                    scale_q("yd", t - 1, y, y, 4, 128)
            project("pn")
            attend("na")

            def low_t(stage, jt, dl, dh, gain=None):
                dve.wait_ge(S(stage, "high"), jt + 1)
                src = PS[:, 6 + jt % 2, :].rearrange("p (c n) -> p c n", c=4)
                if gain is None:
                    i = low(dl, src, dh)
                else:
                    dl2, dh2 = dl, dh.bitcast(F32)
                    i = v.scalar_tensor_tensor(dl2, src, gain, dh2, ALU.mult, ALU.subtract)
                i.then_inc(S(stage, "tev"), 1)

            def merged_low(j):
                t, q = j % NT, j // NT
                dst = (slice(None), slice(4 * q, 4 * q + 4), slice(t * P, (t + 1) * P))
                low_t("o", j, hTl[dst], hTh[dst])

            chunks = [c for c in CHUNKS if c[0] == "g"]
            for c, (_, kind, u0, nu) in enumerate(chunks):
                split_units(u0 + nu + 1)
                for t in range(NT):
                    cols = slice(t * P, (t + 1) * P)
                    if kind == "gate_d0":
                        low_t("g", t, yTl[:, :, cols], yTh[:, :, cols], gains[:, 2:3])
                    elif kind == "gate_n0":
                        low_t("g", NT + t, yTl[:, :, cols], yTh[:, :, cols])
                    elif kind == "gate_n1":
                        merged_low(t)
                if kind[:2] == "br":
                    half = int(kind[4])
                    for t in range(NT):
                        product_done(dve, chunks[c], t)
                        dve.wait_ge(S("g", "sig"), NT * (c // 2) + t + 1)
                        m = mm_[:, t, half * 512:(half + 1) * 512]
                        if kind[3] == "d":
                            v.tensor_tensor(m, m, PS[:, t, :], ALU.mult).then_inc(S("g", "mul"), 1)
                        else:
                            g = sg_n[:, t, :]
                            link(v.tensor_tensor(g, g, PS[:, t, :], ALU.mult))
                            v.tensor_tensor(m, m, g, ALU.add).then_inc(S("g", "mul"), 1)
                        if kind == "br_n1" and t >= 2:
                            merged_low(NT + t - 2)
                split_units(u0 + nu + 2)
            dve.wait_ge(S("g", "mul"), 4 * NT)
            dve.sem_inc(s_phd, 1)
            for j in range(NT + 4, 2 * NT):
                merged_low(j)
            split_units(UNITS)
            dve.wait_ge(S("rt", "g2"), 16)
            for t in range(NT):
                for c in range(2):
                    out_done(dve, t, c)
                    if c == 0:
                        dve.wait_ge(s_x[t], 32)
                    xs = xv[:, t, c * 512:(c + 1) * 512]
                    v.tensor_tensor(xs, xs, PS[:, 2 * (t % 2) + c, :], ALU.add).then_inc(S("o", "added"), 1)
                dve.wait_ge(S("n2", "sq"), t + 1)
                mean_eps(nss[:, t:t + 1], nss[:, t:t + 1], D, S("n2", "ss"))
                dve.wait_ge(S("n2", "rs"), t + 1)
                v.scalar_tensor_tensor(tn[:, t % 2, :], xv[:, t, :], nrs[:, t:t + 1], g2b, ALU.mult, ALU.mult
                                       ).then_inc(S("n2", "hn"), 1)
            dve.wait_ge(S("n2", "hn"), NT)
            dve.sem_inc(x_split, 1)

            def unit_low(e, w):
                n = unit_width(w)
                dve.wait_ge(x_high, e * NXU + w + 1)
                low(xl[:, w % SPLITS, 0:n], xraw[:, w % RAWS, 0:n], xh[:, w % SPLITS, 0:n]).then_inc(x_split, 1)

            dve.wait_ge(S("rt", "logits"), NT)
            lg = PS[:, 6, 0:NT * E].rearrange("p (t e) -> p t e", t=NT)
            v.tensor_copy(aff, lg)
            v.tensor_reduce(rmx, lg, AX.X, ALU.max, negate=True).then_inc(S("rt", "shift"), 1)
            unit_low(0, 0)
            dve.wait_ge(S("rt", "exp"), 1)
            link(v.reciprocal(rrs, rsm))
            v.tensor_tensor(aff, aff, rrs.unsqueeze(2).to_broadcast((P, NT, E)), ALU.mult).then_inc(S("rt", "aff"), 1)
            dve.wait_ge(S("rt", "aff"), 1)
            v.tensor_copy(R[:, :, :, 1], aff)
            link(v.tensor_copy(R[:, :, :, 0], tokid.unsqueeze(2).to_broadcast((P, NT, E))))
            for m in range(3):
                part = R3[:, :, :, m, :]
                i = v.tensor_copy(part, R)
                if m < 2:
                    link(i)
                    link(v.tensor_tensor(R, R, part, ALU.subtract))
            i.then_inc(S("rt", "parts"), 1)
            v.memset(ones, 1.0)
            dve.wait_ge(S("rt", "affT"), 1)
            link(v.tensor_copy(affT[:, 0:512], PS[0:E, 0, :]))
            link(v.tensor_copy(affT[:, 512:768], PS[0:E, 1, 0:256]))
            link(v.tensor_copy(work, affT))
            for lo, hi, cap in ((0, SP_, CP), (SP_, N, CS)):
                for r in range(cap // 8):
                    link(v.max(m8, work[:, lo:hi]))
                    link(v.match_replace(work[:, lo:hi], m8, work[:, lo:hi], -1.0))
            link(v.tensor_tensor(selT, affT, work, ALU.not_equal))
            for lo, hi in ((0, SP_), (SP_, N)):
                link(v.tensor_tensor_scan(cumT[:, lo:hi], ones[:, 0:hi - lo], selT[:, lo:hi], 0.0, ALU.mult, ALU.add))
            v.tensor_tensor(cumT, cumT, selT, ALU.mult).then_inc(S("rt", "rank"), 1)
            dve.wait_ge(S("rt", "rkT"), 1)
            link(v.tensor_copy(rk, PS[:, 7, 0:NT * E].rearrange("p (t e) -> p t e", t=NT)))
            for t in range(NT):
                w = CS if t >= 2 else CP
                if t >= 4:
                    dve.wait_ge(S("rt", "slots"), t - 3)
                v.tensor_tensor(G[:, t % 4, :, 0:w], rk[:, t, :].unsqueeze(2).to_broadcast((P, E, w)),
                                slot1[:, 0:w].unsqueeze(1).to_broadcast((P, E, w)), ALU.is_equal
                                ).then_inc(S("rt", "G"), 1)
            v.memset(idxf[:, 0:1], -1.0)
            v.memset(gate_s[:, 0:1], 0.0)
            v.memset(idxi[:, 0:1], 0)
            for half in range(2):
                i = v.memset(PS[0:CAP, 4 + half, :], 0.0)
            link(i)
            dve.wait_ge(S("rt", "slots"), NT)
            for p0, w, b in ((0, CS, 3), (CS, CP, 2)):
                tab = PS[p0:p0 + w, b, 0:6 * E].rearrange("p (e m c) -> p e c m", m=3, c=2)
                v.tensor_reduce(idxf[p0:p0 + w, 1:E + 1], tab[:, :, 0, :], AX.X, ALU.add)
                i = v.tensor_reduce(gate_s[p0:p0 + w, 1:E + 1], tab[:, :, 1, :], AX.X, ALU.add)
            link(i)
            v.tensor_copy(idxi[:, 1:E + 1], idxf[:, 1:E + 1]).then_inc(S("rt", "tables"), 1)
            dve.wait_ge(S("rt", "tables"), 1)
            dve.sem_inc(s_phd, 1)
            for w in range(1, SPLITS):
                unit_low(0, w)

            def misc_low(what, j, n, n_high, bank):
                dve.wait_ge(S("x", "misc_high"), n_high)
                c0, w = (j * 4 * CAP, 4 * CAP) if what == "tokens" else (HR[j % 3][0] * CAP, HR[j % 3][1] * CAP)
                dh, dl = (xTh, xTl) if what == "tokens" else (hidh, hidl)
                low(dl[:, c0:c0 + w], PS[:, bank, 0:w], dh[:, c0:c0 + w]).then_inc(S("x", "misc_read"), 1)

            def slot_tables(e, val):
                v.tensor_copy(cur_f, idxf[:, bass.ds(e, 1)])
                v.tensor_copy(cur_g, gate_s[:, bass.ds(e, 1)]).then_inc(S("x", "cur"), 1)
                dve.wait_ge(S("x", "cur"), val)
                v.tensor_scalar(scat, iota_tok, cur_f, None, ALU.is_equal).then_inc(S("x", "onehot"), 1)

            def result_low(val):
                dve.wait_ge(S("x", "ye_high"), val)
                for half in range(2):
                    cols = slice(half * 512, (half + 1) * 512)
                    i = v.scalar_tensor_tensor(yel[:, cols], PS[0:CAP, 4 + half, :], cur_g,
                                               yeh[:, cols].bitcast(F32), ALU.mult, ALU.subtract)
                i.then_inc(S("x", "ye_low"), 1)

            dve.wait_ge(S("x", "iota"), 1)
            for q in range(PRE):
                misc_low("tokens", q, q + 1, q + 1, 6 + q)
            highs = [m for _, m in USES if m[0] != "scatter"]

            def expert_body(e, last):
                slot_tables(e, e + 1)
                for u in range(NXU):
                    if u == 0:
                        result_low(e + 1)
                    kind, q, c = XU[u]
                    if kind == "up" and c == 1:
                        dve.wait_ge(x_used, e * NXU + u + 1 + SPLITS)
                        dve.wait_ge(S("x", "silu"), e * 4 + q + 1)
                        h0 = (q % 2) * QF
                        v.tensor_tensor(hid[:, h0:h0 + QF].rearrange("p (h f) -> p h f", h=2),
                                        sg.rearrange("p (h f) -> p h f", h=2), PS[0:CAP, 2:4, 0:QC], ALU.mult
                                        ).then_inc(S("x", "hidden"), 1)
                    for what, j in MISC.get(u, []):
                        n = use_no(what, j)
                        if what == "scatter":
                            t, half = divmod(j, 2)
                            dve.wait_ge(S("x", "misc"), e * NU + PRE + n + 1)
                            xs = xv[:, t, half * 512:(half + 1) * 512]
                            v.tensor_tensor(xs, xs, PS[:, 6 + n % 2, :], ALU.add).then_inc(S("x", "misc_read"), 1)
                        else:
                            misc_low(what, j, e * NU + PRE + n + 1, e * NH_ + PRE + highs.index((what, j)) + 1,
                                     6 + n % 2)
                    w = u + SPLITS
                    if w < NXU:
                        unit_low(e, w)
                    elif not last:
                        unit_low(e + 1, w - NXU)

            with dve.Fori(0, E - 1) as e:
                expert_body(e, False)
            expert_body(E - 1, True)
            slot_tables(E, E + 1)
            result_low(E + 1)
            for j in range(12):
                t, half = divmod(j, 2)
                dve.wait_ge(S("x", "misc"), E * NU + PRE + j + 1)
                xs = xv[:, t, half * 512:(half + 1) * 512]
                i = v.tensor_tensor(xs, xs, PS[:, 6 + j % 2, :], ALU.add)
                i.then_inc(S("x", "misc_read"), 1)
                dve.wait_ge(S("x", "misc_read"), E * NU + PRE + j + 1)
                dve.sem_inc(S("x", "last_added"), 1)


_INS = ["x_prompt", "x_sample", "norm1_g", "w_in", "diff_q_norm", "diff_k_norm", "lambda_q1", "lambda_k1",
        "lambda_q2", "lambda_k2", "diff_subln_g", "rel_bias", "na_q_norm", "na_k_norm", "na_rpb", "w_branch_diff",
        "w_branch_na", "w_out", "norm2_g", "w_router", "w_expert_gate", "w_expert_up", "w_expert_down"]
_KEEP2D = {"norm1_g", "norm2_g", "diff_q_norm", "diff_k_norm", "lambda_q1", "lambda_k1", "lambda_q2", "lambda_k2",
           "diff_subln_g", "rel_bias", "na_q_norm", "na_k_norm"}


def _constants():
    import numpy as np
    c = np.zeros((P, C_W), np.float32)
    c[:, C_ID:C_ID + 128] = np.eye(P)
    col = np.arange(P) % 64
    start = np.clip(col - 8, 0, 48)[:, None]
    kc = np.arange(64)[None, :]
    c[:, C_MASK:C_MASK + 64] = np.where((kc >= start) & (kc < start + 16), 0.0, -1e30)
    c[:, C_TOK:C_TOK + NT] = np.arange(NT)[None, :] * P + np.arange(P)[:, None]
    c[:, C_SLOT:C_SLOT + 64] = 1 + np.arange(64)
    c[:, C_POW:C_POW + 64] = -0.5
    rel = np.arange(1024) - 511
    n = np.abs(rel)
    f = np.float32
    large = 8 + (np.log(np.maximum(n, 1).astype(f) / f(8)) / f(math.log(16.0)) * f(8)).astype(np.int32)
    bucket = np.where(rel > 0, 16, 0) + np.where(n < 8, n, np.minimum(large, 15))
    onehot = (np.arange(32)[:, None] == bucket[None, :]).astype(f)
    return c, onehot


def kernel(**inputs):
    import numpy as np
    import concourse.bacc as bacc
    from concourse.bass_utils import run_bass_kernel_spmd

    nc = bacc.Bacc("TRN2", target_bir_lowering=False, num_devices=1)
    arrays, args = {}, []

    def give(name, a):
        arrays[name] = a
        args.append(nc.dram_tensor(name, a.shape, mybir.dt.from_np(a.dtype), kind="ExternalInput").ap())

    for name in _INS:
        a = np.ascontiguousarray(inputs[name])
        give(f"in_{name}", a if name in _KEEP2D else a.reshape(a.shape[1:]))
    cst, onehot = _constants()
    give("in_consts", cst)
    give("in_t5_onehot", onehot)
    args.append(nc.dram_tensor("out_prompt", (SP_, D), F32, kind="ExternalOutput").ap())
    args.append(nc.dram_tensor("out_sample", (SS, D), F32, kind="ExternalOutput").ap())
    encoder(nc, *args)
    r = run_bass_kernel_spmd(nc, [arrays], core_ids=[0])
    out = r.results[0]
    return out["out_prompt"].reshape(1, SP_, D), out["out_sample"].reshape(1, SS, D)
```
